# Optimizing a Trainium2 kernel written in Bass

```python
import math
import jax, jax.numpy as jnp
from jax import lax
import numpy as np

D_MODEL = 1024
BATCH = 1
SEQ = 512
DEPTH = 2
DEC_BATCH = 8
DEC_SEQ = 4
PAST_LEN = 1024
PAGE_SIZE = 128

DN_HEADS = 4
DN_DK = 128
DN_DV = 128
DN_CONV = 4
DN_CHUNK = 64
SW_QHEADS = 8
SW_KVHEADS = 2
SW_HD = 64
SW_GROUP = SW_QHEADS // SW_KVHEADS
WINDOW = 128
DN_QK_W = DN_HEADS * DN_DK
DN_V_W = DN_HEADS * DN_DV
CONV_DIM = 2 * DN_QK_W + DN_V_W
SW_Q_W = SW_QHEADS * SW_HD
SW_KV_W = SW_KVHEADS * SW_HD
MIX_W = DN_V_W + SW_Q_W
OFF_Z = CONV_DIM
OFF_B = OFF_Z + DN_V_W
OFF_A = OFF_B + DN_HEADS
OFF_SQ = OFF_A + DN_HEADS
OFF_SK = OFF_SQ + SW_Q_W
OFF_SV = OFF_SK + SW_KV_W
IN_DIM = OFF_SV + SW_KV_W
PK_HEADS = 8
N_KEYS = 128
N_EXPERTS = N_KEYS * N_KEYS
PK_QDIM = 256
PK_HALF = PK_QDIM // 2
PK_TOPK = 16
PEER_BLOCK = 128
EPS = 1e-6

kernel_name = 'hymba_deltanet_swa_sink_peer_adaln_step'

def _rmsnorm(x, g):
    xf = x.astype(jnp.float32)
    y = xf * lax.rsqrt(jnp.mean(xf * xf, axis=-1, keepdims=True) + EPS)
    return (y * g.astype(jnp.float32)).astype(x.dtype)

def _l2norm(x):
    return x * lax.rsqrt(jnp.sum(x * x, axis=-1, keepdims=True) + EPS)

def _short_conv(u, buf, w):
    L = u.shape[1]
    up = jnp.concatenate([buf.astype(u.dtype), u], axis=1)
    y = sum(up[:, i:i + L] * w[i] for i in range(DN_CONV))
    return jax.nn.silu(y), up[:, L:]

def _gated_delta(q, k, v, beta, g, s0):
    B, L = q.shape[:2]
    C = DN_CHUNK if L % DN_CHUNK == 0 else L
    N = L // C

    def blocks(t):
        t = t.reshape((B, N, C) + t.shape[2:])
        return jnp.moveaxis(t, 3, 1)

    q, k, v, beta, g = (blocks(t) for t in (q, k, v, beta, g))
    gc = jnp.cumsum(g, axis=-1)
    diff = gc[..., :, None] - gc[..., None, :]
    idx = jnp.arange(C)
    causal = idx[:, None] >= idx[None, :]
    strict = idx[:, None] > idx[None, :]
    decay = jnp.where(causal, jnp.exp(jnp.where(causal, diff, 0.0)), 0.0)
    kk = jnp.einsum('bhncd,bhnsd->bhncs', k, k)
    a_mat = jnp.where(strict, beta[..., :, None] * kk * decay, 0.0) + jnp.eye(C, dtype=q.dtype)
    rhs = jnp.concatenate([beta[..., None] * v, (beta * jnp.exp(gc))[..., None] * k], axis=-1)
    sol = lax.linalg.triangular_solve(a_mat, rhs, left_side=True, lower=True, unit_diagonal=True)
    u0, w = sol[..., :DN_DV], sol[..., DN_DV:]
    qk = jnp.einsum('bhncd,bhnsd->bhncs', q, k) * decay
    q_dec = q * jnp.exp(gc)[..., None]
    k_dec = k * jnp.exp(gc[..., -1:] - gc)[..., None]
    c_dec = jnp.exp(gc[..., -1])

    def step(s, xs):
        u0_n, w_n, qk_n, qd_n, kd_n, cd_n = xs
        u = u0_n - jnp.einsum('bhck,bhkv->bhcv', w_n, s)
        o = jnp.einsum('bhck,bhkv->bhcv', qd_n, s) + jnp.einsum('bhcs,bhsv->bhcv', qk_n, u)
        s = cd_n[..., None, None] * s + jnp.einsum('bhck,bhcv->bhkv', kd_n, u)
        return s, o

    xs = tuple(jnp.moveaxis(t, 2, 0) for t in (u0, w, qk, q_dec, k_dec, c_dec))
    s_fin, o = lax.scan(step, s0, xs)
    o = jnp.transpose(o, (1, 0, 3, 2, 4)).reshape(B, L, DN_HEADS, DN_DV)
    return o, s_fin

def _deltanet(proj, conv_buf, s0, conv_w, a_log, dt_bias, norm_g):
    B, L = proj.shape[:2]
    f32 = jnp.float32
    qkv, new_buf = _short_conv(proj[..., :CONV_DIM], conv_buf, conv_w)
    qkv = qkv.astype(f32)
    q = _l2norm(qkv[..., :DN_QK_W].reshape(B, L, DN_HEADS, DN_DK)) * (DN_DK ** -0.5)
    k = _l2norm(qkv[..., DN_QK_W:2 * DN_QK_W].reshape(B, L, DN_HEADS, DN_DK))
    v = qkv[..., 2 * DN_QK_W:].reshape(B, L, DN_HEADS, DN_DV)
    z = proj[..., OFF_Z:OFF_B].astype(f32).reshape(B, L, DN_HEADS, DN_DV)
    beta = jax.nn.sigmoid(proj[..., OFF_B:OFF_A].astype(f32))
    g = -jnp.exp(a_log.astype(f32)) * jax.nn.softplus(proj[..., OFF_A:OFF_SQ].astype(f32) + dt_bias.astype(f32))
    o, s_new = _gated_delta(q, k, v, beta, g, s0.astype(f32))
    o = _rmsnorm(o, norm_g) * jax.nn.silu(z)
    return o.reshape(B, L, DN_V_W).astype(proj.dtype), s_new.astype(s0.dtype), new_buf

def _sink_attend(q, k, v, mask, sinks):
    f32 = jnp.float32
    s = jnp.einsum('...qhgd,...khd->...hgqk', q.astype(f32), k.astype(f32)) * (SW_HD ** -0.5)
    s = jnp.where(mask, s, -jnp.inf)
    sink = jnp.broadcast_to(sinks.astype(f32)[:, :, None, None], s.shape[:-1] + (1,))
    p = jax.nn.softmax(jnp.concatenate([s, sink], axis=-1), axis=-1)[..., :-1]
    return jnp.einsum('...hgqk,...khd->...qhgd', p, v.astype(f32))

def _swa_prompt(q, k, v, sinks):
    B, L = q.shape[:2]
    nb = L // WINDOW
    qb = q.reshape(B, nb, WINDOW, SW_KVHEADS, SW_GROUP, SW_HD)
    kb = k.reshape(B, nb, WINDOW, SW_KVHEADS, SW_HD)
    vb = v.reshape(B, nb, WINDOW, SW_KVHEADS, SW_HD)
    kk = jnp.concatenate([jnp.concatenate([jnp.zeros_like(kb[:, :1]), kb[:, :-1]], axis=1), kb], axis=2)
    vv = jnp.concatenate([jnp.concatenate([jnp.zeros_like(vb[:, :1]), vb[:, :-1]], axis=1), vb], axis=2)
    qpos = WINDOW + jnp.arange(WINDOW)
    kpos = jnp.arange(2 * WINDOW)
    d = qpos[:, None] - kpos[None, :]
    band = (d >= 0) & (d < WINDOW)
    valid = (jnp.arange(nb) > 0)[:, None, None] | (kpos >= WINDOW)[None, None, :]
    mask = (band[None] & valid)[:, None, None]
    o = _sink_attend(qb, kk, vv, mask, sinks)
    return o.reshape(B, L, SW_Q_W)

def _swa_decode(q, k, v, k_buf, v_buf, sinks):
    B, L = q.shape[:2]
    P = k_buf.shape[1]
    kk = jnp.concatenate([k_buf.astype(k.dtype), k], axis=1)
    vv = jnp.concatenate([v_buf.astype(v.dtype), v], axis=1)
    qpos = P + jnp.arange(L)
    kpos = jnp.arange(P + L)
    d = qpos[:, None] - kpos[None, :]
    mask = ((d >= 0) & (d < WINDOW))[None, None, None]
    o = _sink_attend(q.reshape(B, L, SW_KVHEADS, SW_GROUP, SW_HD), kk, vv, mask, sinks)
    return o.reshape(B, L, SW_Q_W), kk[:, L:], vv[:, L:]

def _peer(h, wq, sub_keys, u_tab, v_tab):
    B, L, D = h.shape
    T = B * L
    f32 = jnp.float32
    xf = h.reshape(T, D)
    q = (xf @ wq).reshape(T, PK_HEADS, 2, PK_HALF).astype(f32)
    s = jnp.einsum('thpd,hpnd->thpn', q, sub_keys.astype(f32))
    s1, i1 = lax.top_k(s[:, :, 0], PK_TOPK)
    s2, i2 = lax.top_k(s[:, :, 1], PK_TOPK)
    cand = (s1[..., :, None] + s2[..., None, :]).reshape(T, PK_HEADS, PK_TOPK * PK_TOPK)
    cidx = (i1[..., :, None] * N_KEYS + i2[..., None, :]).reshape(T, PK_HEADS, PK_TOPK * PK_TOPK)
    top_s, pos = lax.top_k(cand, PK_TOPK)
    eidx = jnp.take_along_axis(cidx, pos, axis=-1).reshape(T, PK_HEADS * PK_TOPK)
    gate = jax.nn.softmax(top_s, axis=-1).reshape(T, PK_HEADS * PK_TOPK)
    nblk = -(-T // PEER_BLOCK)
    pad = nblk * PEER_BLOCK - T
    xb = jnp.pad(xf, ((0, pad), (0, 0))).reshape(nblk, PEER_BLOCK, D)
    ib = jnp.pad(eidx, ((0, pad), (0, 0))).reshape(nblk, PEER_BLOCK, PK_HEADS * PK_TOPK)
    gb = jnp.pad(gate, ((0, pad), (0, 0))).reshape(nblk, PEER_BLOCK, PK_HEADS * PK_TOPK)

    def block(args):
        xt, it, gt = args
        a = jnp.einsum('td,tkd->tk', xt.astype(f32), u_tab[it].astype(f32))
        a = jax.nn.gelu(a, approximate=False) * gt
        return jnp.einsum('tk,tkd->td', a, v_tab[it].astype(f32))

    out = lax.map(block, (xb, ib, gb)).reshape(nblk * PEER_BLOCK, D)[:T]
    return out.reshape(B, L, D).astype(h.dtype)

def _layer(x, c, prior, norm1_g, norm2_g, w_ada, b_ada, w_in, conv_w, dn_a_log,
           dn_dt_bias, dn_norm_g, sw_sinks, w_out, peer_wq, peer_keys, peer_u, peer_v):
    B, L, _ = x.shape
    mod = jax.nn.silu(c.astype(jnp.float32)) @ w_ada.astype(jnp.float32) + b_ada.astype(jnp.float32)
    sh1, sc1, g1, sh2, sc2, g2 = [m[:, None, :].astype(x.dtype) for m in jnp.split(mod, 6, axis=-1)]
    h = _rmsnorm(x, norm1_g) * (1 + sc1) + sh1
    proj = h @ w_in
    if prior is None:
        conv_buf = jnp.zeros((B, DN_CONV - 1, CONV_DIM), proj.dtype)
        s0 = jnp.zeros((B, DN_HEADS, DN_DK, DN_DV), x.dtype)
    else:
        s0, conv_buf, k_buf, v_buf = prior
    o_dn, new_s, new_conv = _deltanet(proj, conv_buf, s0, conv_w, dn_a_log, dn_dt_bias, dn_norm_g)
    q = proj[..., OFF_SQ:OFF_SK]
    k = proj[..., OFF_SK:OFF_SV].reshape(B, L, SW_KVHEADS, SW_HD)
    v = proj[..., OFF_SV:IN_DIM].reshape(B, L, SW_KVHEADS, SW_HD)
    sinks = sw_sinks.reshape(SW_KVHEADS, SW_GROUP)
    if prior is None:
        o_sw = _swa_prompt(q, k, v, sinks)
        n_buf = min(WINDOW, PAST_LEN)
        new_k, new_v = k[:, L - n_buf:], v[:, L - n_buf:]
    else:
        o_sw, new_k, new_v = _swa_decode(q, k, v, k_buf, v_buf, sinks)
    mix = jnp.concatenate([o_dn, o_sw.astype(x.dtype)], axis=-1) @ w_out
    x = x + g1 * mix
    h2 = _rmsnorm(x, norm2_g) * (1 + sc2) + sh2
    x = x + g2 * _peer(h2, peer_wq, peer_keys, peer_u, peer_v)
    return x, (new_s, new_conv, new_k, new_v)

def _trunk(x, c, prior_stack, layer_params, final_norm_g):
    new = []
    for l in range(DEPTH):
        prior = None if prior_stack is None else tuple(s[l] for s in prior_stack)
        x, st = _layer(x, c, prior, *[a[l] for a in layer_params])
        new.append(st)
    y = _rmsnorm(x, final_norm_g)
    return y, [jnp.stack(z) for z in zip(*new)]

def setup_inputs(seed: int = 0) -> dict:
    key = jax.random.key(seed)
    ks = jax.random.split(key, 26)
    f32 = jnp.float32

    def nrm(k, shape, scale):
        return jax.random.normal(k, shape, f32) * scale

    n_buf = min(WINDOW, PAST_LEN)
    dt = jnp.exp(jax.random.uniform(ks[20], (DEPTH, DN_HEADS), f32, math.log(1e-3), math.log(1e-1)))
    return {
        'x_prompt': nrm(ks[0], (BATCH, SEQ, D_MODEL), 1.0),
        'x_sample': nrm(ks[1], (DEC_BATCH, DEC_SEQ, D_MODEL), 1.0),
        'state_delta': nrm(ks[2], (DEPTH, DEC_BATCH, DN_HEADS, DN_DK, DN_DV), 0.05),
        'state_conv': nrm(ks[3], (DEPTH, DEC_BATCH, DN_CONV - 1, CONV_DIM), 1.0),
        'cache_swa_k': nrm(ks[4], (DEPTH, DEC_BATCH, n_buf, SW_KVHEADS, SW_HD), 1.0),
        'cache_swa_v': nrm(ks[5], (DEPTH, DEC_BATCH, n_buf, SW_KVHEADS, SW_HD), 1.0),
        'c_prompt': nrm(ks[6], (BATCH, D_MODEL), 1.0),
        'c_sample': nrm(ks[7], (DEC_BATCH, D_MODEL), 1.0),
        'norm1_g': 1.0 + nrm(ks[8], (DEPTH, D_MODEL), 0.02),
        'norm2_g': 1.0 + nrm(ks[9], (DEPTH, D_MODEL), 0.02),
        'final_norm_g': 1.0 + nrm(ks[10], (D_MODEL,), 0.02),
        'w_ada': nrm(ks[11], (DEPTH, D_MODEL, 6 * D_MODEL), 0.5 * D_MODEL ** -0.5),
        'b_ada': nrm(ks[12], (DEPTH, 6 * D_MODEL), 0.01),
        'w_in': nrm(ks[13], (DEPTH, D_MODEL, IN_DIM), D_MODEL ** -0.5),
        'conv_w': nrm(ks[14], (DEPTH, DN_CONV, CONV_DIM), DN_CONV ** -0.5),
        'dn_a_log': jnp.log(jax.random.uniform(ks[15], (DEPTH, DN_HEADS), f32, 1.0, 16.0)),
        'dn_dt_bias': dt + jnp.log(-jnp.expm1(-dt)),
        'dn_norm_g': 1.0 + nrm(ks[16], (DEPTH, DN_DV), 0.02),
        'sw_sinks': nrm(ks[17], (DEPTH, SW_QHEADS), 0.5),
        'w_out': nrm(ks[18], (DEPTH, MIX_W, D_MODEL), MIX_W ** -0.5),
        'peer_wq': nrm(ks[19], (DEPTH, D_MODEL, PK_HEADS * PK_QDIM), D_MODEL ** -0.5),
        'peer_keys': nrm(ks[21], (DEPTH, PK_HEADS, 2, N_KEYS, PK_HALF), PK_HALF ** -0.5),
        'peer_u': nrm(ks[22], (DEPTH, N_EXPERTS, D_MODEL), D_MODEL ** -0.5),
        'peer_v': nrm(ks[23], (DEPTH, N_EXPERTS, D_MODEL), 0.5),
    }

def reference(x_prompt, x_sample, state_delta, state_conv, cache_swa_k, cache_swa_v,
              c_prompt, c_sample, norm1_g, norm2_g, final_norm_g, w_ada, b_ada, w_in,
              conv_w, dn_a_log, dn_dt_bias, dn_norm_g, sw_sinks, w_out, peer_wq,
              peer_keys, peer_u, peer_v):
    layer_params = (norm1_g, norm2_g, w_ada, b_ada, w_in, conv_w, dn_a_log, dn_dt_bias,
                    dn_norm_g, sw_sinks, w_out, peer_wq, peer_keys, peer_u, peer_v)
    y_prompt, (delta_p, conv_p, k_p, v_p) = _trunk(x_prompt, c_prompt, None, layer_params, final_norm_g)
    y_sample, (delta_s, conv_s, k_s, v_s) = _trunk(
        x_sample, c_sample, (state_delta, state_conv, cache_swa_k, cache_swa_v), layer_params, final_norm_g)
    return (y_prompt, y_sample, delta_p, conv_p, k_p, v_p, delta_s, conv_s, k_s, v_s)


_drawn_inputs = setup_inputs


def setup_inputs(seed=0):
    import zlib

    import numpy as np

    out = dict(_drawn_inputs(seed))
    spreads = {}
    factors = {'norm2_g': 3.242,
     'final_norm_g': 2.912,
     'b_ada': 2.787,
     'dn_norm_g': 6.074,
     'sw_sinks': 8.0}
    for name, (base, spread) in spreads.items():
        noise = np.random.default_rng([zlib.crc32(name.encode()), seed]).standard_normal(out[name].shape)
        drawn = base * np.exp(spread * noise) if base else spread * noise
        out[name] = __import__('jax').numpy.asarray(drawn.astype(out[name].dtype))
    for name, factor in factors.items():
        out[name] = (out[name] * factor).astype(out[name].dtype)
    return out
```

```python
from contextlib import ExitStack

import concourse.bass as bass
from concourse import mybir

F32 = mybir.dt.float32
U32 = mybir.dt.uint32
ALU = mybir.AluOpType
ACT = mybir.ActivationFunctionType
AX = mybir.AxisListType.X

P = 128
L = 2
D = 1024
KC = D // P
TILES = 4
UNITS = TILES + 1
NB, SLOTS = 8, 16
HIST = 3
H = 4
CH = 12
QH, HD = 8, 64
NKEY = 128
PKH = 8
TOPK = 16
NEXP = NKEY * NKEY
EXPERTS = PKH * TOPK
EPS = 1e-6
MISC = 264
LEVELS = 7
G = 4
PG = EXPERTS // G
SG = PG // 4
LG = TILES * PG + SG

CHUNKS = ["mod_a", "conv0", "conv1", "conv2", "swq", "z", "misc", "state", "cache",
          "wo0", "wo1", "mod_b", "wq0", "wq1", "wq2", "wq3", "keys"]
BIG = {"conv0": 0, "conv1": 1, "conv2": 2, "swq": 3, "z": 4, "wo0": 5, "wo1": 6,
       "wq0": 7, "wq1": 8, "wq2": 9, "wq3": 10}

PER_UNIT = dict(
    x_in=16, masks_in=16, x_stored=32, h_normed=1, hT_ps=2, hT_sb=2, conv_ps=3, uT_sb=1, swq_ps=1, swq_sb=1,
    z_ps=1, z_sb=1, misc_ps=1, misc_sb=1, conv_sum=1, conv_silu=1, tail_kept=1, dt_in=1, gb_act=1,
    qkv_ps=3, qkv_sb=3, qk_normed=1, qkT_ps=2, qkT_sb=2, grow=1, g_ps=1, gcol_sb=1, diff_sb=1,
    decay_sb=1, kk_ps=1, at_sb=1, level_b=LEVELS, u1_ps=LEVELS, u1_sb=LEVELS, xu_ps=LEVELS,
    x_level=LEVELS, ks_ps=1, rhs_sb=1, u_ps=1, u_sb=1, o_ps=1, dn_done=1,
    sc_ps=1, sc_max=1, sc_exp=1, pT_ps=4, pT_sb=4, pv_ps=1, mix_sb=1, kv_kept=1,
    mixT_ps=2, mixT_sb=2, wo_ps=2, h2_sb=1, h2T_ps=2, h2T_sb=2, wq_ps=4, wq_sb=4, keys_ps=4,
    keys_sb=4, square_sb=5, root_sb=5, top_sub=1, top_exp=1, topk_sb=1, acc_ps=1, x_out=1, y_out=1)
AHEAD = dict(x_stored=32, tail_kept=1, kv_kept=1)
DVE_STEPS = {"prompt": 64, "batch": 66}
ACT_STEPS = {"prompt": 1, "batch": 2}


def trunk(nc, ins, outs):
    with ExitStack() as ctx:
        def sb(name, shape, dt=F32):
            return ctx.enter_context(nc.sbuf_tensor(name, shape, dt))

        def ps(name, shape):
            return ctx.enter_context(nc.psum_tensor(name, shape, F32))

        def sem(name):
            return ctx.enter_context(nc.semaphore(name))

        W = sb("W", [P, 2, 4096])
        ubuf = sb("ubuf", [P, 2, G, D])
        vbuf = sb("vbuf", [P, 2, G, D])
        x = sb("x", [P, D])
        h = sb("h", [P, D])
        hz = sb("hz", [P, 2 * NB * 144])
        h2, g2 = hz[:, 0:D], hz[:, D:2 * D]
        Z = hz[:, :].rearrange("p (i z) -> p i z", i=2)
        gfin = sb("gfin", [P, D])
        hT = sb("hT", [P, KC, P])
        uT = sb("uT", [P, CH, HIST + P])
        qkvT = sb("qkvT", [P, CH, P])
        qkv = sb("qkv", [P, CH, P])
        decay = sb("decay", [P, H, P])
        AT = sb("AT", [P, H, P])
        X = sb("X", [P, H, P])
        XT = sb("XT", [P, H, P])
        BT = sb("BT", [P, H, P])
        U1 = sb("U1", [P, H, P])
        QK = sb("QK", [P, H, P])
        S = sb("S", [P, H, P])
        z = sb("z", [P, H * P])
        mix = sb("mix", [P, D])
        swqT = sb("swqT", [P, 4, P])
        kcat = sb("kcat", [P, 2, P])
        kvtok = sb("kvtok", [P, 2, 2 * P])
        J = sb("J", [P, 2, 2048])
        cw = sb("cw", [P, CH, 4])
        hist = sb("hist", [P, CH, NB, HIST])
        tails = sb("tails", [P, CH, NB, HIST])
        small = sb("small", [P, 256])
        v16 = sb("v16", [P, PKH, 2, TOPK])
        i16 = sb("i16", [P, PKH, 2, TOPK], U32)
        if16 = sb("if16", [P, PKH, 2, TOPK])
        ts16 = sb("ts16", [P, PKH, TOPK])
        pos = sb("pos", [P, PKH, TOPK], U32)
        pi = sb("pi", [P, 2, EXPERTS], U32)
        pf = sb("pf", [P, 2, EXPERTS])
        gate = sb("gate", [P, EXPERTS])
        idx = sb("idx", [P, EXPERTS], U32)
        idxu = sb("idxu", [P, 2, G], U32)
        idxv = sb("idxv", [P, 2, G], U32)
        a4 = sb("a4", [P, 2, 3, G])
        diag = sb("diag", [P, 2, G, P])
        ident = sb("ident", [P, P])
        zeros = sb("zeros", [P, P])
        ones = sb("ones", [P, P])
        sel = sb("sel", [P, P])
        masks = sb("masks", [P, 2 * P + 2 * P + LEVELS * P + 1 + NB])
        iota = sb("iota", [P, TOPK])
        lcon = sb("lcon", [P, 4 + 4 + 8 + P + 1])

        causal = masks[:, 0:P]
        strict = masks[:, P:2 * P]
        swmask = masks[:, 2 * P:4 * P]
        level = [masks[:, (4 + i) * P:(5 + i) * P] for i in range(LEVELS)]
        valid = masks[:, (4 + LEVELS) * P:(4 + LEVELS) * P + 1]
        rowmask = masks[:, (4 + LEVELS) * P + 1:(4 + LEVELS) * P + 1 + NB]
        a_log, dt_bias, sinks = lcon[:, 0:4], lcon[:, 4:8], lcon[:, 8:16]
        norm_g, idx_off = lcon[:, 16:16 + P], lcon[:, 16 + P:17 + P]

        at_ = [0]

        def sm(n):
            at_[0] += n
            return small[:, at_[0] - n:at_[0]]
        ss, rs = sm(1), sm(1)
        rn, ab, ta, tabs, trel = sm(8), sm(8), sm(4), sm(4), sm(4)
        e4, l4, g4, beta, expa = sm(4), sm(4), sm(4), sm(4), sm(4)
        gcol, egc, be, dl, r4 = sm(4), sm(4), sm(4), sm(4), sm(4)
        cdec, mx, es, rl = sm(32), sm(8), sm(8), sm(8)

        B = [ps(f"B{i}", [P, 512]) for i in range(6)]
        ACC = [ps(f"ACC{i}", [P, 512]) for i in range(2)]

        s = {n: sem(n) for n in PER_UNIT}
        w_in = {c: sem("in_" + c) for c in CHUNKS}
        const_in, gfin_in, cst, sel_in = sem("const_in"), sem("gfin_in"), sem("cst"), sem("sel_in")
        layer_in, reset, p_stored = sem("layer_in"), sem("reset"), sem("p_stored")
        hist_in, z_made, z_used = sem("hist_in"), sem("z_made"), sem("z_used")
        sup_ps, sup_sb, s_stored = sem("sup_ps"), sem("sup_sb"), sem("s_stored")
        sup_sb_rows = sem("sup_sb_rows")
        z_clear = sem("z_clear")
        tails_sb, tails_stored = sem("tails_sb"), sem("tails_stored")
        bounce_out, bounce_in, cache_out = sem("bounce_out"), sem("bounce_in"), sem("cache_out")
        x0_in = sem("x0_in")
        dve_order, act_order, pool_order, settled = sem("dve_order"), sem("act_order"), sem("pool_order"), sem("settled")
        u_in = [sem(f"u_in{i}") for i in range(2)]
        v_in = [sem(f"v_in{i}") for i in range(2)]
        dots, gelu_sb, ag_sb, diag_sb, v_acc = sem("dots"), sem("gelu_sb"), sem("ag_sb"), sem("diag_sb"), sem("v_acc")
        c_in, wa_in, ba_in = sem("c_in"), [sem("wa_in0"), sem("wa_in1")], sem("ba_in")
        c_silu, mod_ps, mod_sum, mod_sb, mod_out = sem("c_silu"), sem("mod_ps"), sem("mod_sum"), sem("mod_sb"), sem("mod_out")

        V, A, T = nc.vector, nc.scalar, nc.tensor

        def spread(ap, n):
            return ap.unsqueeze(2).to_broadcast([P, ap.shape[1], n])

        def again(ap, n):
            return ap.unsqueeze(1).to_broadcast([P, n, ap.shape[1]])

        def wslot(chunk):
            return W[:, CHUNKS.index(chunk) % 2, :]

        def blocks(chunk):
            return wslot(chunk).rearrange("p (j k n) -> p j k n", j=4, k=KC)

        def cols(chunk):
            return wslot(chunk).rearrange("p (k n) -> p k n", k=KC)

        misc_w = wslot("misc")[:, 0:KC * MISC].rearrange("p (k n) -> p k n", k=KC)
        keys_w = wslot("keys")[:, 0:2048].rearrange("p (j n) -> p j n", j=16)
        SS = wslot("state").rearrange("p (b h d) -> p b h d", b=NB, h=H)
        KcT = wslot("cache")[:, 0:1024].rearrange("p (b n) -> p b n", b=NB)
        Vc = wslot("cache")[:, 1024:2048].rearrange("p (b n) -> p b n", b=NB)
        sh1, A1 = wslot("mod_a")[:, 0:D], wslot("mod_a")[:, D:2 * D]
        g1, sh2, A2 = (wslot("mod_b")[:, i * D:(i + 1) * D] for i in range(3))
        Zd = [Z[:, i, :].rearrange("p (b k) -> p b k", k=144)[:, :, 0:SLOTS] for i in range(2)]
        Zm = [Z[:, i, 0:NB * P].rearrange("p (b k) -> p b k", b=NB) for i in range(2)]
        sc = J[:, 0, :]
        sc2 = J[:, 1, :]
        PT = J[:, 1, :].rearrange("p (j n) -> p j n", j=16)
        qpT = PT
        ET = U1
        R = BT
        h3 = lambda ap: ap.rearrange("p (h n) -> p h n", h=H)
        arena = ubuf[:, :, :, :].rearrange("p a g d -> p (a g d)")
        mod9 = arena[0:9, 0:6 * D]
        bada9 = vbuf[0:9, :, :, :].rearrange("p a g d -> p (a g d)")[:, 0:6 * D]
        ng9 = hz[0:9, 0:D]
        ng9b = hz[0:9, D:2 * D]
        cT = small[:, 128:128 + 72]

        block = ctx.enter_context(nc.Block())

        def units(eng, body, before=None, after=None, end=None):
            with eng.Fori(0, L) as layer:
                if before:
                    before(layer)
                with eng.Fori(0, TILES) as tile:
                    body("prompt", layer, tile, layer * UNITS + tile)
                if after:
                    after(layer)
                body("batch", layer, TILES, layer * UNITS + TILES)

        def waiter(eng, u):
            def wait(name, n):
                eng.wait_ge(s[name], u * PER_UNIT[name] + AHEAD.get(name, 0) + n)
            return wait

        @block.sync
        def _(sp):
            def settle():
                sp.sem_inc(settled, 1)

            sp.dma_start(outs["xbuf"][0], ins["xs"]).then_inc(x0_in, 16)
            sp.dma_start(cT, ins["cT"]).then_inc(c_in, 16)
            sp.dma_start(ident[:], ins["ident"]).then_inc(const_in, 16)
            sp.dma_start(iota[:], ins["iota"]).then_inc(const_in, 16)
            sp.dma_start(sel[:], ins["sel"]).then_inc(sel_in, 16)
            sp.dma_start(gfin[:], ins["gfin"].partition_broadcast(P)).then_inc(gfin_in, 16)
            for l in range(L):
                if l:
                    sp.wait_ge(mod_out, 16 * l)
                    settle()
                sp.dma_start(bada9, ins["b_ada"][l].partition_broadcast(9)).then_inc(ba_in, 16)
                sp.dma_start(ng9, ins["g1n"][l].partition_broadcast(9)).then_inc(ba_in, 16)
                sp.dma_start(ng9b, ins["g2n"][l].partition_broadcast(9)).then_inc(ba_in, 16)
                for j in range(12):
                    n = 12 * l + j
                    if n >= 2:
                        sp.wait_ge(mod_ps, n - 1)
                    sp.dma_start(W[:, n % 2, :], ins["w_ada"][l, j]).then_inc(wa_in[n % 2], 16)
                sp.wait_ge(mod_sb, l + 1)
                sp.dma_start(outs["mod"][l], mod9).then_inc(mod_out, 16)
            sp.wait_ge(mod_out, 16 * L)
            sp.wait_ge(x0_in, 16)

            def layer_start(layer):
                sp.wait_ge(s["x_stored"], 32 + layer * UNITS * 32)
                settle()
                sp.dma_start(lcon[:], ins["lcon"][layer]).then_inc(layer_in, 16)
                sp.dma_start(cw[:], ins["cw"][layer]).then_inc(layer_in, 16)
                sp.dma_start(hist[:], ins["hist"][layer]).then_inc(layer_in, 16)

            def prompt_end(layer):
                sp.wait_ge(s["x_stored"], 32 + (layer * UNITS + TILES) * 32)
                settle()
                sp.wait_ge(s["tail_kept"], 1 + layer * UNITS + TILES)
                settle()
                sp.wait_ge(s["kv_kept"], 1 + layer * UNITS + TILES)
                settle()
                sp.dma_start(outs["delta_p"][layer], S[:]).then_inc(p_stored, 16)
                sp.dma_start(outs["conv_p"][layer], uT[:, :, 0:HIST]).then_inc(p_stored, 16)
                sp.dma_start(outs["kv_p"][layer], kvtok[:, 0, :]).then_inc(p_stored, 16)

            def unit(kind, layer, tile, u):
                wait = waiter(sp, u)
                batch = kind == "batch"
                wait("x_stored", 0)
                settle()
                sp.dma_start(x[:], outs["xbuf"][layer, tile]).then_inc(s["x_in"], 16)
                sp.dma_start(masks[:], ins["masks"][tile]).then_inc(s["masks_in"], 16)
                freed = dict(mod_a=("h_normed", 1), conv0=("conv_ps", 1), conv1=("conv_ps", 2),
                             conv2=("conv_ps", 3), swq=("swq_ps", 1), z=("z_ps", 1),
                             misc=("misc_ps", 1), wo0=("wo_ps", 1), wo1=("wo_ps", 2),
                             mod_b=("h2_sb", 1), wq0=("wq_ps", 1), wq1=("wq_ps", 2),
                             wq2=("wq_ps", 3), wq3=("wq_ps", 4), keys=("keys_ps", 4))
                last = {0: None, 1: None}
                for c in CHUNKS:
                    i = CHUNKS.index(c) % 2
                    if c in ("state", "cache") and not batch:
                        continue
                    if last[i] == "state":
                        sp.wait_ge(s_stored, 16 * (layer + 1))
                        settle()
                    elif last[i] == "cache":
                        wait("pv_ps", 1)
                        settle()
                    elif last[i]:
                        wait(*freed[last[i]])
                        settle()
                    last[i] = c
                    if c in BIG:
                        dst, src = wslot(c), ins["w_big"][layer, BIG[c]]
                    elif c == "misc":
                        dst, src = wslot(c)[:, 0:KC * MISC], ins["w_misc"][layer]
                    elif c == "keys":
                        dst, src = wslot(c)[:, 0:2048], ins["keysT"][layer]
                    elif c == "state":
                        dst, src = SS, ins["state"][layer]
                    elif c == "cache":
                        dst, src = wslot(c)[:, 0:2048], ins["cache"][layer]
                    else:
                        rows = (0, 2) if c == "mod_a" else (2, 5)
                        n = (rows[1] - rows[0]) * D
                        dst = wslot(c)[:, 0:n]
                        src = mod_rows(layer, batch, rows[0] * D, n)
                    if c == "mod_b":
                        sp.dma_start(g2, mod_rows(layer, batch, 5 * D, D)).then_inc(w_in[c], 16)
                    sp.dma_start(dst, src).then_inc(w_in[c], 16)
                    if c == "cache":
                        sp.wait_ge(sup_sb, 4 * (layer + 1))
                        settle()
                        sp.dma_start(outs["delta_s"][layer], SS).then_inc(s_stored, 16)
                if batch:
                    sp.wait_ge(tails_sb, layer + 1)
                    settle()
                    sp.dma_start(outs["conv_s"][layer], tails[:]).then_inc(tails_stored, 16)
                    for n, cache in enumerate(("k", "v")):
                        sp.dma_start(outs[cache + "_s"][layer, :, 0:P - 4, :],
                                     ins["cache_" + cache][layer, :, 4:P, :]).then_inc(cache_out, 16)
                        for b in range(NB):
                            lo = SLOTS * b + HIST
                            sp.dma_start(outs[cache + "_s"][layer, b, P - 4:P, :],
                                         kvtok[lo:lo + 4, 1, n * P:(n + 1) * P]).then_inc(cache_out, 16)
                    wait("topk_sb", 1)
                    settle()
                    sp.dma_start(outs["b_idx"], idx[:]).then_inc(bounce_out, 16)
                    sp.dma_start(outs["b_gate"], gate[:]).then_inc(bounce_out, 16)
                    sp.dma_start(outs["b_h2"], h2).then_inc(bounce_out, 16)
                    sp.wait_ge(bounce_out, 48 * (layer + 1))
                    settle()
                    tok = "(b s) k -> b s k"
                    EQ = EXPERTS // 4
                    for q in range(4):
                        for b in range(NB):
                            lo = 32 * q + 4 * b
                            r = slice(SLOTS * b + HIST, SLOTS * b + HIST + 4)
                            sp.dma_start(idx[lo:lo + 4, 0:EQ], outs["b_idx"][r, EQ * q:EQ * q + EQ]).then_inc(bounce_in, 16)
                            sp.dma_start(gate[lo:lo + 4, 0:EQ], outs["b_gate"][r, EQ * q:EQ * q + EQ]).then_inc(bounce_in, 16)
                            sp.dma_start(h2[lo:lo + 4, :], outs["b_h2"][r, :]).then_inc(bounce_in, 16)
                wait("x_out", 1)
                settle()
                sp.dma_start(outs["xbuf"][layer + 1, tile], x[:]).then_inc(s["x_stored"], 16)
                wait("y_out", 1)
                settle()
                sp.dma_start(outs["y"][layer, tile], h[:]).then_inc(s["x_stored"], 16)

            def mod_rows(layer, batch, lo, n):
                m = outs["mod"][layer, :, lo:lo + n]
                if batch:
                    return m[1:9].unsqueeze(1).to_broadcast([NB, SLOTS, n])
                return m[0].partition_broadcast(P)

            units(sp, unit, layer_start, prompt_end)
            sp.wait_ge(s["x_stored"], 32 + 32 * L * UNITS)
            sp.wait_ge(p_stored, 48 + 48 * L)
            sp.wait_ge(s_stored, 16 * L)
            sp.wait_ge(tails_stored, 16 + 16 * L)
            sp.wait_ge(cache_out, 16 * 18 * (L + 1))

        @block.gpsimd
        def _(pool):
            g = nc.gpsimd
            g.memset(zeros[:], 0.0)
            g.memset(ones[:], 1.0).then_inc(cst, 1)
            pool.wait_ge(cst, 1)

            def settle():
                pool.sem_inc(settled, 1)

            def layer_start(layer):
                pool.wait_ge(p_stored, 48 + 48 * layer)
                pool.wait_ge(s["x_stored"], 32 + 32 * UNITS * layer)
                settle()
                g.tensor_copy(uT[:, :, 0:HIST], zeros[:, 0:CH * HIST].rearrange("p (c t) -> p c t", c=CH))
                g.tensor_copy(kcat[:, 0, :], zeros[:])
                g.tensor_copy(kvtok[:, 0, 0:P], zeros[:])
                g.tensor_copy(kvtok[:, 0, P:2 * P], zeros[:])
                for hh in range(H):
                    last = g.tensor_copy(S[:, hh, :], zeros[:])
                last.then_inc(reset, 1)

            def unit(kind, layer, tile, u):
                wait = waiter(pool, u)
                batch = kind == "batch"
                nx = [0]
                if batch:
                    wait("x_stored", 0)
                    settle()
                    g.memset(hz[:], 0.0).then_inc(z_clear, 1)
                    pool.wait_ge(p_stored, 48 + 48 * (layer + 1))
                    wait("uT_sb", 1)
                    src = uT[:, :, HIST:HIST + P].rearrange("p c (b t) -> p c b t", b=NB)
                    pool.wait_ge(tails_stored, 16 + 16 * layer)
                    settle()
                    g.tensor_copy(tails[:], src[:, :, :, HIST + 1:HIST + 4]).then_inc(tails_sb, 1)
                wait("conv_sum", 1)
                settle()
                g.tensor_copy(uT[:, :, 0:HIST], uT[:, :, P:P + HIST]).then_inc(s["tail_kept"], 1)

                def expand(src):
                    n = nx[0]
                    if n >= 2:
                        pool.wait_ge(z_used, 20 * layer + n - 1)
                    settle()
                    g.tensor_copy(Zd[n % 2], src.rearrange("p (b t) -> p b t", b=NB)).then_inc(z_made, 1)
                    nx[0] += 1
                if batch:
                    wait("qkT_sb", 2)
                    pool.wait_ge(z_clear, layer + 1)
                    for hh in range(H):
                        expand(qkvT[:, 4 + hh, :])
                    for hh in range(H):
                        expand(qkvT[:, hh, :])
                    for hb in range(4):
                        expand(swqT[:, hb, :])
                    for hh in range(QH):
                        wait("pT_sb", hh // 2 + 1)
                        expand(PT[:, 2 * hh, :])
                wait("pv_ps", 1)
                settle()
                g.tensor_copy(kcat[:, 0, :], kcat[:, 1, :])
                g.tensor_copy(kvtok[:, 0, :], kvtok[:, 1, :]).then_inc(s["kv_kept"], 1)
                if batch:
                    pool.wait_ge(bounce_in, 16 * 96 * (layer + 1))
                else:
                    wait("topk_sb", 1)
                groups = SG if batch else PG
                first = layer * LG + tile * PG
                settle()
                with pool.Fori(0, groups // 2) as i:
                    for par in range(2):
                        n = first + i * 2 + par
                        pool.wait_ge(dots, n + 1)
                        settle()
                        now = idx[:, bass.ds(i * (2 * G) + par * G, G)]
                        g.tensor_copy(idxu[:, par, :], now).then_inc(pool_order, 1)
                        pool.wait_ge(pool_order, n * 2 + 1)
                        settle()
                        for j in range(G):
                            off = bass.IndirectOffsetOnAxis(ap=idxu[:, par, j:j + 1], axis=0)
                            g.indirect_dma_start(out=ubuf[:, par, j, :], out_offset=None, in_=ins["peer_u"],
                                                 in_offset=off).then_inc(u_in[par], 16)
                        pool.wait_ge(v_acc, n + 1)
                        settle()
                        g.tensor_copy(idxv[:, par, :], now).then_inc(pool_order, 1)
                        pool.wait_ge(pool_order, n * 2 + 2)
                        settle()
                        for j in range(G):
                            off = bass.IndirectOffsetOnAxis(ap=idxv[:, par, j:j + 1], axis=0)
                            g.indirect_dma_start(out=vbuf[:, par, j, :], out_offset=None, in_=ins["peer_v"],
                                                 in_offset=off).then_inc(v_in[par], 16)

            units(pool, unit, layer_start)

        @block.scalar
        def _(act):
            state = {"base": 0, "n": 0}

            def link(instruction):
                state["n"] += 1
                instruction.then_inc(act_order, 1)
                act.wait_ge(act_order, state["base"] + state["n"])

            act.wait_ge(c_in, 16)
            A.activation(cT, cT, ACT.Silu).then_inc(c_silu, 1)

            def unit(kind, layer, tile, u):
                wait = waiter(act, u)
                batch = kind == "batch"
                a, b = ACT_STEPS["prompt"], ACT_STEPS["batch"]
                state["base"] = layer * (TILES * a + b) + tile * a
                state["n"] = 0

                def root(nth, ap):
                    wait("square_sb", nth)
                    A.activation(ap, ap, ACT.Sqrt).then_inc(s["root_sb"], 1)
                root(1, ss)
                for i in range(2):
                    wait("hT_ps", i + 1)
                    A.copy(hT[:, 4 * i:4 * i + 4, :], B[i][:].rearrange("p (j n) -> p j n", j=4)).then_inc(s["hT_sb"], 1)
                wait("tail_kept", 0)
                for i in range(3):
                    wait("conv_ps", i + 1)
                    last = A.copy(uT[:, 4 * i:4 * i + 4, HIST:HIST + P], B[2 + i][:].rearrange("p (j n) -> p j n", j=4))
                if batch:
                    act.wait_ge(layer_in, 48 * (layer + 1))
                    link(last)
                    dst = uT[:, :, HIST:HIST + P].rearrange("p c (b t) -> p c b t", b=NB)[:, :, :, 0:HIST]
                    last = A.copy(dst, hist[:])
                last.then_inc(s["uT_sb"], 1)
                wait("swq_ps", 1)
                A.mul(swqT[:], B[5][:].rearrange("p (j n) -> p j n", j=4), HD ** -0.5).then_inc(s["swq_sb"], 1)
                wait("z_ps", 1)
                A.activation(z[:], B[0][:], ACT.Silu).then_inc(s["z_sb"], 1)
                wait("misc_ps", 1)
                wait("kv_kept", 0)
                act.wait_ge(reset, layer + 1)
                act.wait_ge(cache_out, 16 * 18 * (layer + 1))
                A.copy(kcat[:, 1, :], B[1][:, MISC:MISC + P])
                A.copy(kvtok[:, 1, :], B[1][:, 0:2 * P])
                A.copy(ab, B[1][:, 2 * P:MISC]).then_inc(s["misc_sb"], 1)
                wait("conv_sum", 1)
                A.activation(qkvT[:], qkvT[:], ACT.Silu).then_inc(s["conv_silu"], 1)
                wait("dt_in", 1)
                link(A.activation(e4, tabs, ACT.Exp, scale=-1.0))
                A.activation(expa, a_log, ACT.Exp)
                A.activation(l4, e4, ACT.Ln, bias=1.0)
                A.activation(beta, ab[:, 0:4], ACT.Sigmoid).then_inc(s["gb_act"], 1)
                for i in range(3):
                    wait("qkv_ps", i + 1)
                    A.copy(qkv[:, 4 * i:4 * i + 4, :], B[2 + i][:].rearrange("p (j n) -> p j n", j=4)).then_inc(s["qkv_sb"], 1)
                root(2, rn)
                for i in range(2):
                    wait("qkT_ps", i + 1)
                    A.copy(qkvT[:, 4 * i:4 * i + 4, :], B[i][:].rearrange("p (j n) -> p j n", j=4)).then_inc(s["qkT_sb"], 1)
                wait("g_ps", 1)
                A.copy(gcol, B[5][:, 0:4])
                A.activation(egc, B[5][:, 0:4], ACT.Exp)
                if batch:
                    ends = B[2][:].rearrange("p (g t) -> p g t", t=SLOTS)[:, :, SLOTS - 1]
                    last = A.activation(cdec, ends, ACT.Exp)
                else:
                    last = A.activation(cdec[:, 0:H], h3(B[2][:])[:, :, P - 1], ACT.Exp)
                last.then_inc(s["gcol_sb"], 1)
                wait("diff_sb", 1)
                A.activation(decay[:], decay[:], ACT.Exp).then_inc(s["decay_sb"], 1)
                for i in range(LEVELS):
                    wait("u1_ps", i + 1)
                    A.copy(U1[:], h3(B[0][:])).then_inc(s["u1_sb"], 1)
                wait("u_ps", 1)
                A.copy(ET[:], h3(B[0][:])).then_inc(s["u_sb"], 1)
                root(3, r4)
                wait("sc_max", 1)
                A.activation(sc, sc, ACT.Exp)
                A.activation(es, es, ACT.Exp).then_inc(s["sc_exp"], 1)
                for i in range(4):
                    wait("pT_ps", i + 1)
                    A.copy(PT[:, 4 * i:4 * i + 4, :], B[(4, 5, 0, 1)[i]][:].rearrange("p (j n) -> p j n", j=4)).then_inc(s["pT_sb"], 1)
                for i in range(2):
                    wait("mixT_ps", i + 1)
                    A.copy(hT[:, 4 * i:4 * i + 4, :], B[3 + i][:].rearrange("p (j n) -> p j n", j=4)).then_inc(s["mixT_sb"], 1)
                root(4, ss)
                for i in range(2):
                    wait("h2T_ps", i + 1)
                    A.copy(hT[:, 4 * i:4 * i + 4, :], B[2 + i][:].rearrange("p (j n) -> p j n", j=4)).then_inc(s["h2T_sb"], 1)
                for i in range(4):
                    wait("wq_ps", i + 1)
                    A.copy(qpT[:, 4 * i:4 * i + 4, :], B[(4, 5, 0, 1)[i]][:].rearrange("p (j n) -> p j n", j=4)).then_inc(s["wq_sb"], 1)
                for i in range(4):
                    wait("keys_ps", i + 1)
                    A.copy(sc[:, 512 * i:512 * i + 512], B[2 + i][:]).then_inc(s["keys_sb"], 1)
                wait("top_sub", 1)
                A.activation(gate[:], gate[:], ACT.Exp).then_inc(s["top_exp"], 1)
                groups = SG if batch else PG
                first = layer * LG + tile * PG
                pick = sel if batch else ident
                with act.Fori(0, groups // 2) as i:
                    for par in range(2):
                        n = first + i * 2 + par
                        act.wait_ge(dots, n + 3)
                        A.activation(a4[:, par, 1, :], a4[:, par, 0, :], ACT.Gelu).then_inc(gelu_sb, 1)
                        act.wait_ge(ag_sb, n + 1)
                        act.wait_ge(v_acc, n + 1)
                        for j in range(G):
                            last = A.activation(diag[:, par, j, :], pick[:], ACT.Copy, scale=a4[:, par, 2, j:j + 1])
                        last.then_inc(diag_sb, 1)
                root(5, ss)
                if batch:
                    assert state["n"] == b, ("ACT batch", state["n"])
                else:
                    assert state["n"] == a, ("ACT prompt", state["n"])

            act.wait_ge(const_in, 32)
            act.wait_ge(sel_in, 16)
            units(act, unit)

        @block.vector
        def _(dve):
            state = {"base": 0, "n": 0}

            def link(instruction):
                state["n"] += 1
                instruction.then_inc(dve_order, 1)
                dve.wait_ge(dve_order, state["base"] + state["n"])

            def settle():
                dve.sem_inc(settled, 1)

            dve.sem_inc(dots, 2)
            dve.sem_inc(v_acc, 2)
            for name, n in AHEAD.items():
                dve.sem_inc(s[name], n)
            dve.sem_inc(p_stored, 48)
            dve.sem_inc(tails_stored, 16)
            dve.sem_inc(cache_out, 16 * 18)
            for l in range(L):
                dve.wait_ge(ba_in, 48 * (l + 1))
                for j in range(12):
                    dve.wait_ge(mod_ps, 12 * l + j + 1)
                    last = V.tensor_tensor(mod9[:, 512 * j:512 * j + 512], B[j % 2][0:9, :],
                                           bada9[:, 512 * j:512 * j + 512], ALU.add)
                    if j < 11:
                        last.then_inc(mod_sum, 1)
                last.then_inc(mod_sum, 1)
                dve.wait_ge(mod_sum, 12 * (l + 1))
                m = mod9
                V.scalar_tensor_tensor(m[:, D:2 * D], m[:, D:2 * D], 1.0, ng9, ALU.add, ALU.mult)
                V.scalar_tensor_tensor(m[:, 4 * D:5 * D], m[:, 4 * D:5 * D], 1.0, ng9b, ALU.add, ALU.mult).then_inc(mod_sb, 1)

            def norm(wait, nth, src, out, gain, shift):
                link(V.tensor_tensor_reduce(out, src, src, 1.0, 0.0, ALU.mult, ALU.add, ss))
                V.tensor_scalar(ss, ss, 1.0 / D, EPS, ALU.mult, ALU.add).then_inc(s["square_sb"], 1)
                wait("root_sb", nth)
                link(V.reciprocal(rs, ss))
                last = V.scalar_tensor_tensor(out, src, rs, gain, ALU.mult, ALU.mult)
                if shift is not None:
                    link(last)
                    last = V.tensor_tensor(out, out, shift, ALU.add)
                return last

            def unit(kind, layer, tile, u):
                wait = waiter(dve, u)
                batch = kind == "batch"
                a, b = DVE_STEPS["prompt"], DVE_STEPS["batch"]
                state["base"] = layer * (TILES * a + b) + tile * a
                state["n"] = 0
                wait("x_in", 16)
                dve.wait_ge(w_in["mod_a"], 16 * (u + 1))
                wait("x_stored", 0)
                norm(wait, 1, x[:], h[:], A1, sh1).then_inc(s["h_normed"], 1)
                wait("uT_sb", 1)
                dve.wait_ge(reset, layer + 1)
                dve.wait_ge(layer_in, 48 * (layer + 1))
                wait("masks_in", 16)
                tmp = sc[:, 0:CH * P].rearrange("p (c t) -> p c t", c=CH)
                link(V.tensor_tensor(qkvT[:], uT[:, :, 0:P], spread(cw[:, :, 0], P), ALU.mult))
                for i in range(1, 4):
                    link(V.tensor_tensor(tmp, uT[:, :, i:i + P], spread(cw[:, :, i], P), ALU.mult))
                    last = V.tensor_tensor(qkvT[:], qkvT[:], tmp, ALU.add)
                    if i < 3:
                        link(last)
                last.then_inc(s["conv_sum"], 1)
                wait("misc_sb", 1)
                link(V.tensor_tensor(ta, ab[:, 4:8], dt_bias, ALU.add))
                V.tensor_scalar(trel, ta, 0.0, None, ALU.max)
                V.scalar_tensor_tensor(tabs, ta, -1.0, ta, ALU.mult, ALU.max).then_inc(s["dt_in"], 1)
                wait("gb_act", 1)
                link(V.tensor_tensor(g4, l4, trel, ALU.add))
                link(V.scalar_tensor_tensor(g4, g4, -1.0, expa, ALU.mult, ALU.mult))
                V.tensor_scalar(g4, g4, valid, None, ALU.mult)
                link(V.tensor_scalar(beta, beta, valid, None, ALU.mult))
                for hh in range(H):
                    V.tensor_scalar(X[:, hh, :], causal, g4[:, hh:hh + 1], None, ALU.mult)
                    last = V.tensor_scalar(XT[:, hh, :], ident[:], beta[:, hh:hh + 1], None, ALU.mult)
                last.then_inc(s["grow"], 1)
                wait("qkv_sb", 3)
                qk = qkv[:, 0:8, :]
                sq = sc[:, 0:8 * P].rearrange("p (c t) -> p c t", c=8)
                link(V.tensor_tensor(sq, qk, qk, ALU.mult))
                link(V.tensor_reduce(rn, sq, AX, ALU.add))
                V.tensor_scalar(rn, rn, EPS, None, ALU.add).then_inc(s["square_sb"], 1)
                wait("root_sb", 2)
                link(V.reciprocal(rn, rn))
                link(V.tensor_scalar(rn[:, 0:4], rn[:, 0:4], P ** -0.5, None, ALU.mult))
                V.tensor_tensor(qk, qk, spread(rn, P), ALU.mult).then_inc(s["qk_normed"], 1)
                wait("g_ps", 1)
                wait("gcol_sb", 1)
                for hh in range(H):
                    last = V.tensor_scalar(decay[:, hh, :], h3(B[2][:])[:, hh, :], gcol[:, hh:hh + 1], 0.0, ALU.subtract, ALU.min)
                last.then_inc(s["diff_sb"], 1)
                wait("decay_sb", 1)
                link(V.tensor_tensor(decay[:], decay[:], again(causal, H), ALU.mult))
                wait("kk_ps", 1)
                link(V.tensor_tensor(AT[:], h3(B[4][:]), decay[:], ALU.mult))
                link(V.tensor_tensor(AT[:], AT[:], again(strict, H), ALU.mult))
                link(V.tensor_tensor(AT[:], AT[:], h3(B[3][:]), ALU.mult))
                V.tensor_tensor(QK[:], h3(B[1][:]), decay[:], ALU.mult)
                V.tensor_tensor(qkv[:, 8:12, :], qkv[:, 8:12, :], spread(beta, P), ALU.mult)
                V.scalar_tensor_tensor(be, beta, -1.0, egc, ALU.mult, ALU.mult)
                V.tensor_copy(X[:], again(ident[:], H))
                V.tensor_copy(XT[:], again(ident[:], H))
                if batch:
                    ends = decay[:].rearrange("p h (b t) -> p h b t", t=SLOTS)[:, :, :, SLOTS - 1]
                    link(V.tensor_reduce(dl, ends, AX, ALU.add))
                else:
                    link(V.tensor_copy(dl, decay[:, :, P - 1]))
                wait("qkT_sb", 2)
                V.tensor_tensor(qkv[:, 4:8, :], qkv[:, 4:8, :], spread(dl, P), ALU.mult).then_inc(s["at_sb"], 1)
                for i in range(LEVELS):
                    V.tensor_tensor(BT[:], AT[:], again(level[i], H), ALU.mult).then_inc(s["level_b"], 1)
                    wait("xu_ps", i + 1)
                    V.tensor_tensor(X[:], X[:], h3(B[2][:]), ALU.subtract)
                    V.tensor_tensor(XT[:], XT[:], h3(B[3][:]), ALU.subtract).then_inc(s["x_level"], 1)
                    wait("x_level", i + 1)
                wait("ks_ps", 1)
                link(V.tensor_tensor(R[:], h3(B[4][:]), spread(be, P), ALU.mult))
                V.tensor_tensor(R[:], R[:], qkv[:, 8:12, :], ALU.add).then_inc(s["rhs_sb"], 1)
                od = h3(mix[:, 0:H * P])
                link(V.tensor_tensor(od, h3(B[5][:]), spread(egc, P), ALU.mult))
                wait("o_ps", 1)
                link(V.tensor_tensor(od, od, h3(B[1][:]), ALU.add))
                if batch:
                    dve.wait_ge(w_in["state"], 16 * (layer + 1))
                    for hh in range(H):
                        if hh >= 2:
                            dve.wait_ge(sup_ps, 4 * layer + hh - 1)
                        kd = sc2 if hh % 2 else sc
                        V.tensor_tensor(kd[:, 0:NB * P].rearrange("p (b d) -> p b d", b=NB),
                                        again(qkv[:, 4 + hh, :], NB), spread(rowmask, P), ALU.mult).then_inc(sup_sb_rows, 1)
                        link(V.tensor_tensor(SS[:, :, hh, :], SS[:, :, hh, :], spread(cdec[:, NB * hh:NB * hh + NB], P), ALU.mult))
                        dve.wait_ge(sup_ps, 4 * layer + hh + 1)
                        V.tensor_tensor(SS[:, 0:4, hh, :], SS[:, 0:4, hh, :], h3(B[2][:]), ALU.add)
                        V.tensor_tensor(SS[:, 4:8, hh, :], SS[:, 4:8, hh, :], h3(B[3][:]), ALU.add).then_inc(sup_sb, 1)
                    last = None
                else:
                    link(V.tensor_tensor(S[:], S[:], spread(cdec[:, 0:H], P), ALU.mult))
                    link(V.tensor_tensor(S[:], S[:], h3(B[2][:]), ALU.add))
                wait("z_sb", 1)
                sq = sc[:, 0:H * P].rearrange("p (c t) -> p c t", c=H)
                if batch:
                    dve.wait_ge(sup_ps, 4 * layer + 4)
                link(V.tensor_tensor(sq, od, od, ALU.mult))
                link(V.tensor_reduce(r4, sq, AX, ALU.add))
                V.tensor_scalar(r4, r4, 1.0 / P, EPS, ALU.mult, ALU.add).then_inc(s["square_sb"], 1)
                wait("root_sb", 3)
                link(V.reciprocal(r4, r4))
                link(V.tensor_tensor(od, od, spread(r4, P), ALU.mult))
                link(V.tensor_tensor(od, od, again(norm_g, H), ALU.mult))
                V.tensor_tensor(mix[:, 0:H * P], mix[:, 0:H * P], z[:], ALU.mult).then_inc(s["dn_done"], 1)
                wait("sc_ps", 1)
                for i in range(4):
                    last = V.tensor_tensor(sc[:, 512 * i:512 * i + 512].rearrange("p (h k) -> p h k", h=2),
                                           B[i][:].rearrange("p (h k) -> p h k", h=2), again(swmask, 2), ALU.add)
                link(last)
                sc3 = sc.rearrange("p (h k) -> p h k", h=QH)
                link(V.tensor_reduce(mx, sc3, AX, ALU.max))
                link(V.tensor_tensor(mx, mx, sinks, ALU.max))
                V.tensor_tensor(es, sinks, mx, ALU.subtract)
                V.tensor_tensor(sc3, sc3, spread(mx, 2 * P), ALU.subtract).then_inc(s["sc_max"], 1)
                wait("sc_exp", 1)
                link(V.tensor_reduce(rl, sc3, AX, ALU.add))
                link(V.tensor_tensor(rl, rl, es, ALU.add))
                link(V.reciprocal(rl, rl))
                wait("pv_ps", 1)
                V.tensor_tensor(mix[:, H * P:].rearrange("p (h d) -> p h d", h=QH),
                                B[2][:].rearrange("p (h d) -> p h d", h=QH), spread(rl, HD), ALU.mult).then_inc(s["mix_sb"], 1)
                wait("wo_ps", 2)
                dve.wait_ge(w_in["mod_b"], 32 * (u + 1))
                for i in range(2):
                    last = V.tensor_tensor(h[:, 512 * i:512 * i + 512], B[i][:], g1[:, 512 * i:512 * i + 512], ALU.mult)
                link(last)
                link(V.tensor_tensor(x[:], x[:], h[:], ALU.add))
                norm(wait, 4, x[:], h2, A2, sh2).then_inc(s["h2_sb"], 1)
                wait("keys_sb", 4)

                def best16(src, spare, vals, idxs, rows, n):
                    row = lambda ap, j: ap[:, n * j:n * j + n]
                    settle()
                    for j in range(rows):
                        last = V.max(vals[:, j, 0:8], row(src, j))
                    link(last)
                    settle()
                    for j in range(rows):
                        V.max_index(idxs[:, j, 0:8], vals[:, j, 0:8], row(src, j))
                        last = V.match_replace(row(spare, j), vals[:, j, 0:8], row(src, j), -3e38)
                    link(last)
                    settle()
                    for j in range(rows):
                        last = V.max(vals[:, j, 8:16], row(spare, j))
                    link(last)
                    settle()
                    for j in range(rows):
                        last = V.max_index(idxs[:, j, 8:16], vals[:, j, 8:16], row(spare, j))
                    link(last)
                best16(sc, sc2, v16[:].rearrange("p h s k -> p (h s) k"), i16[:].rearrange("p h s k -> p (h s) k"), 16, P)
                sums = sc.rearrange("p (h i j) -> p h i j", h=PKH, i=TOPK)
                V.tensor_copy(if16[:], i16[:])
                for hh in range(PKH):
                    last = V.tensor_tensor(sums[:, hh], spread(v16[:, hh, 0, :], TOPK), again(v16[:, hh, 1, :], TOPK), ALU.add)
                link(last)
                best16(sc, sc2, ts16[:], pos[:], PKH, TOPK * TOPK)
                V.tensor_tensor(gate[:].rearrange("p (h k) -> p h k", h=PKH), ts16[:],
                                spread(ts16[:, :, 0], TOPK), ALU.subtract).then_inc(s["top_sub"], 1)
                posf = pos[:].rearrange("p h k -> p (h k)")
                V.tensor_scalar(pi[:, 0, :], posf, 4, None, ALU.logical_shift_right)
                link(V.tensor_scalar(pi[:, 1, :], posf, 15, None, ALU.bitwise_and))
                link(V.tensor_copy(pf[:], pi[:]))
                hot = [sc.rearrange("p (k j) -> p k j", j=TOPK), sc2.rearrange("p (k j) -> p k j", j=TOPK)]
                for i in range(2):
                    last = V.tensor_tensor(hot[i], spread(pf[:, i, :], TOPK), again(iota[:], EXPERTS), ALU.is_equal)
                link(last)
                for i in range(2):
                    for hh in range(PKH):
                        k = slice(TOPK * hh, TOPK * hh + TOPK)
                        last = V.tensor_tensor(hot[i][:, k, :], hot[i][:, k, :], again(if16[:, hh, i, :], TOPK), ALU.mult)
                link(last)
                for i in range(2):
                    last = V.tensor_reduce(pf[:, i, :], hot[i], AX, ALU.add)
                link(last)
                link(V.scalar_tensor_tensor(pf[:, 0, :], pf[:, 0, :], float(NKEY), pf[:, 1, :], ALU.mult, ALU.add))
                link(V.tensor_scalar(pf[:, 0, :], pf[:, 0, :], idx_off, None, ALU.add))
                V.tensor_copy(idx[:], pf[:, 0, :])
                wait("top_exp", 1)
                g3 = gate[:].rearrange("p (h k) -> p h k", h=PKH)
                link(V.tensor_reduce(rn, g3, AX, ALU.add))
                link(V.reciprocal(rn, rn))
                V.tensor_tensor(g3, g3, spread(rn, TOPK), ALU.mult).then_inc(s["topk_sb"], 1)
                wait("topk_sb", 1)
                if batch:
                    dve.wait_ge(bounce_in, 16 * 96 * (layer + 1))
                groups = SG if batch else PG
                first = layer * LG + tile * PG
                settle()
                with dve.Fori(0, groups // 2) as i:
                    for par in range(2):
                        n = first + i * 2 + par
                        rows = layer * (LG // 2) + tile * (PG // 2) + i + 1
                        dve.wait_ge(u_in[par], rows * (16 * G))
                        for j in range(G):
                            last = V.tensor_tensor_reduce(ubuf[:, par, j, :], ubuf[:, par, j, :], h2, 1.0, 0.0,
                                                          ALU.mult, ALU.add, a4[:, par, 0, j:j + 1])
                        last.then_inc(dots, 1)
                        dve.wait_ge(gelu_sb, n + 1)
                        V.tensor_tensor(a4[:, par, 2, :], a4[:, par, 1, :],
                                        gate[:, bass.ds(i * (2 * G) + par * G, G)], ALU.mult).then_inc(ag_sb, 1)
                wait("acc_ps", 1)
                for i in range(2):
                    last = V.tensor_tensor(h[:, 512 * i:512 * i + 512], ACC[i][:], g2[:, 512 * i:512 * i + 512], ALU.mult)
                link(last)
                V.tensor_tensor(x[:], x[:], h[:], ALU.add).then_inc(s["x_out"], 1)
                wait("x_out", 1)
                norm(wait, 5, x[:], h[:], gfin[:], None).then_inc(s["y_out"], 1)
                assert state["n"] == (b if batch else a), ("DVE", kind, state["n"])

            dve.wait_ge(const_in, 32)
            dve.wait_ge(gfin_in, 16)
            units(dve, unit)

        @block.tensor
        def _(pe):
            pe.wait_ge(c_silu, 1)
            cT3 = cT.rearrange("p (k c) -> p k c", k=KC)
            for n in range(12 * L):
                pe.wait_ge(wa_in[n % 2], 16 * (n // 2 + 1))
                if n >= 2:
                    pe.wait_ge(mod_sum, n - 1)
                w = W[:, n % 2, :].rearrange("p (k n) -> p k n", k=KC)
                for k in range(KC):
                    last = T.matmul(B[n % 2][0:9, :], cT3[:, k, :], w[:, k, :], start=(k == 0), stop=(k == KC - 1))
                last.then_inc(mod_ps, 1)

            def turn(src, banks, name, wait_for):
                for i, bank in enumerate(banks):
                    wait_for(i)
                    for j in range(4):
                        last = T.transpose(bank[:, P * j:P * j + P], src(4 * i + j), ident[:])
                    last.then_inc(s[name], 1)

            def unit(kind, layer, tile, u):
                wait = waiter(pe, u)
                batch = kind == "batch"
                nz = [0]
                none = lambda i: None

                def chunk(c):
                    n = layer + 1 if c in ("state", "cache") else u + 1
                    pe.wait_ge(w_in[c], 16 * n)

                def expanded(out, rhs, start, stop, done=True):
                    n = nz[0]
                    pe.wait_ge(z_made, 20 * layer + n + 1)
                    for b in range(NB):
                        last = T.matmul(out, Zm[n % 2][:, b, :], rhs(b), start=start and b == 0, stop=stop and b == NB - 1)
                    last.then_inc(z_used, 1)
                    nz[0] += 1

                wait("h_normed", 1)
                turn(lambda j: h[:, P * j:P * j + P], B[0:2], "hT_ps", none)
                wait("hT_sb", 2)
                for i, c in enumerate(("conv0", "conv1", "conv2", "swq")):
                    chunk(c)
                    for j in range(4):
                        for k in range(KC):
                            last = T.matmul(B[2 + i][:, P * j:P * j + P], blocks(c)[:, j, k, :], hT[:, k, :],
                                            start=(k == 0), stop=(k == KC - 1))
                    last.then_inc(s["conv_ps" if i < 3 else "swq_ps"], 1)
                chunk("z")
                for k in range(KC):
                    last = T.matmul(B[0][:], hT[:, k, :], cols("z")[:, k, :], start=(k == 0), stop=(k == KC - 1))
                last.then_inc(s["z_ps"], 1)
                chunk("misc")
                for k in range(KC):
                    T.matmul(B[1][:, 0:MISC], hT[:, k, :], misc_w[:, k, :], start=(k == 0), stop=(k == KC - 1))
                for k in range(KC):
                    last = T.matmul(B[1][:, MISC:MISC + P], misc_w[:, k, 0:P], hT[:, k, :], start=(k == 0), stop=(k == KC - 1))
                last.then_inc(s["misc_ps"], 1)
                wait("conv_silu", 1)
                turn(lambda j: qkvT[:, j, :], B[2:5], "qkv_ps", none)
                wait("qk_normed", 1)
                wait("z_sb", 1)
                wait("misc_sb", 1)
                turn(lambda j: qkv[:, j, :], B[0:2], "qkT_ps", none)
                wait("grow", 1)
                wait("qkv_sb", 3)
                wait("swq_sb", 1)
                T.matmul(B[2][:], ones[:], X[:].rearrange("p h n -> p (h n)"), start=True, stop=True)
                T.matmul(B[5][:, 0:4], causal, g4, start=True, stop=True)
                T.matmul(B[3][:], ones[:], XT[:].rearrange("p h n -> p (h n)"), start=True, stop=True).then_inc(s["g_ps"], 1)
                wait("qkT_sb", 2)
                for hh in range(H):
                    T.matmul(B[4][:, P * hh:P * hh + P], qkvT[:, 4 + hh, :], qkvT[:, 4 + hh, :], start=True, stop=True)
                for hh in range(H):
                    last = T.matmul(B[1][:, P * hh:P * hh + P], qkvT[:, 4 + hh, :], qkvT[:, hh, :], start=True, stop=True)
                last.then_inc(s["kk_ps"], 1)
                wait("at_sb", 1)
                for i in range(LEVELS):
                    wait("level_b", i + 1)
                    for hh in range(H):
                        last = T.matmul(B[0][:, P * hh:P * hh + P], BT[:, hh, :], X[:, hh, :], start=True, stop=True)
                    last.then_inc(s["u1_ps"], 1)
                    wait("u1_sb", i + 1)
                    for hh in range(H):
                        T.matmul(B[2][:, P * hh:P * hh + P], XT[:, hh, :], U1[:, hh, :], start=True, stop=True)
                        last = T.matmul(B[3][:, P * hh:P * hh + P], U1[:, hh, :], XT[:, hh, :], start=True, stop=True)
                    last.then_inc(s["xu_ps"], 1)
                if batch:
                    chunk("state")
                    for bank in (B[4], B[5]):
                        for hh in range(H):
                            expanded(bank[:, P * hh:P * hh + P], lambda b: SS[:, b, hh, :], True, True)
                    wait("x_level", LEVELS)
                    last = T.matmul(B[0][:, 0:4], zeros[:], g4, start=True, stop=True)
                else:
                    for hh in range(H):
                        T.matmul(B[4][:, P * hh:P * hh + P], qkvT[:, 4 + hh, :], S[:, hh, :], start=True, stop=True)
                    for hh in range(H):
                        last = T.matmul(B[5][:, P * hh:P * hh + P], qkvT[:, hh, :], S[:, hh, :], start=True, stop=True)
                last.then_inc(s["ks_ps"], 1)
                wait("rhs_sb", 1)
                wait("x_level", LEVELS)
                for hh in range(H):
                    last = T.matmul(B[0][:, P * hh:P * hh + P], XT[:, hh, :], R[:, hh, :], start=True, stop=True)
                last.then_inc(s["u_ps"], 1)
                wait("u_sb", 1)
                for hh in range(H):
                    last = T.matmul(B[1][:, P * hh:P * hh + P], QK[:, hh, :], ET[:, hh, :], start=True, stop=True)
                if batch:
                    last.then_inc(s["o_ps"], 1)
                    for hh in range(H):
                        pe.wait_ge(sup_sb_rows, 4 * layer + hh + 1)
                        if hh:
                            pe.wait_ge(sup_sb, 4 * layer + hh)
                        kd = (sc2 if hh % 2 else sc)[:, 0:NB * P].rearrange("p (b d) -> p b d", b=NB)
                        for b in range(NB):
                            last = T.matmul(B[2 + b // 4][:, P * (b % 4):P * (b % 4) + P], kd[:, b, :], ET[:, hh, :],
                                            start=True, stop=True)
                        last.then_inc(sup_ps, 1)
                else:
                    for hh in range(H):
                        last = T.matmul(B[2][:, P * hh:P * hh + P], qkv[:, 4 + hh, :], ET[:, hh, :], start=True, stop=True)
                    last.then_inc(s["o_ps"], 1)
                wait("dn_done", 1)
                wait("swq_sb", 1)
                if batch:
                    chunk("cache")
                for hb in range(4):
                    for kv in range(2):
                        hh = 4 * kv + hb
                        rows = slice(HD * kv, HD * kv + HD)
                        out = B[hh // 2][:, 2 * P * (hh % 2):2 * P * (hh % 2) + 2 * P]
                        if batch:
                            n = nz[0]
                            if kv == 0:
                                pe.wait_ge(z_made, 20 * layer + n + 1)
                            for b in range(NB):
                                last = T.matmul(out[:, 0:P], Zm[n % 2][rows, b, :], KcT[rows, b, :], start=b == 0, stop=b == NB - 1)
                            if kv == 1:
                                last.then_inc(z_used, 1)
                                nz[0] += 1
                            last = T.matmul(out[:, P:2 * P], swqT[rows, hb, :], kcat[rows, 1, :], start=True, stop=True)
                        else:
                            last = T.matmul(out, swqT[rows, hb, :], kcat[rows, :, :].rearrange("p a n -> p (a n)"), start=True, stop=True)
                last.then_inc(s["sc_ps"], 1)
                wait("sc_exp", 1)
                turn(lambda j: sc[:, P * j:P * j + P], [B[4], B[5], B[0], B[1]], "pT_ps", none)
                for hh in range(QH):
                    wait("pT_sb", hh // 2 + 1)
                    vcol = P + HD * (hh // 4)
                    out = B[2][:, HD * hh:HD * hh + HD]
                    T.matmul(out, PT[:, 2 * hh + 1, :], kvtok[:, 1, vcol:vcol + HD], start=True, stop=False)
                    if batch:
                        expanded(out, lambda b: Vc[:, b, vcol - P:vcol - P + HD], False, True)
                    else:
                        last = T.matmul(out, PT[:, 2 * hh, :], kvtok[:, 0, vcol:vcol + HD], start=False, stop=True)
                if batch:
                    last = T.matmul(B[3][:, 0:4], zeros[:], g4, start=True, stop=True)
                last.then_inc(s["pv_ps"], 1)
                wait("mix_sb", 1)
                turn(lambda j: mix[:, P * j:P * j + P], B[3:5], "mixT_ps", none)
                wait("mixT_sb", 2)
                for i in range(2):
                    chunk(f"wo{i}")
                    for k in range(KC):
                        last = T.matmul(B[i][:], hT[:, k, :], cols(f"wo{i}")[:, k, :], start=(k == 0), stop=(k == KC - 1))
                    last.then_inc(s["wo_ps"], 1)
                wait("h2_sb", 1)
                turn(lambda j: h2[:, P * j:P * j + P], B[2:4], "h2T_ps", none)
                wait("h2T_sb", 2)
                for i in range(4):
                    chunk(f"wq{i}")
                    for j in range(4):
                        for k in range(KC):
                            last = T.matmul(B[(4, 5, 0, 1)[i]][:, P * j:P * j + P], blocks(f"wq{i}")[:, j, k, :], hT[:, k, :],
                                            start=(k == 0), stop=(k == KC - 1))
                    last.then_inc(s["wq_ps"], 1)
                chunk("keys")
                wait("wq_sb", 4)
                for i in range(4):
                    for j in range(4):
                        jj = 4 * i + j
                        last = T.matmul(B[2 + i][:, P * j:P * j + P], qpT[:, jj, :], keys_w[:, jj, :], start=True, stop=True)
                    last.then_inc(s["keys_ps"], 1)
                for i in range(2):
                    T.matmul(ACC[i][:], zeros[:], ident[:].unsqueeze(1).to_broadcast([P, 4, P]), start=True, stop=False, skip_group_check=True)
                groups = SG if batch else PG
                first = layer * LG + tile * PG
                with pe.Fori(0, groups // 2) as i:
                    for par in range(2):
                        n = first + i * 2 + par
                        rows = layer * (LG // 2) + tile * (PG // 2) + i + 1
                        pe.wait_ge(diag_sb, n + 1)
                        pe.wait_ge(v_in[par], rows * (16 * G))
                        for j in range(G):
                            for c in range(2):
                                last = T.matmul(ACC[c][:], diag[:, par, j, :], vbuf[:, par, j, 512 * c:512 * c + 512],
                                                start=False, stop=False, skip_group_check=True)
                        last.then_inc(v_acc, 1)
                for i in range(2):
                    last = T.matmul(ACC[i][:], zeros[:], ident[:].unsqueeze(1).to_broadcast([P, 4, P]),
                                    start=False, stop=True, skip_group_check=True)
                last.then_inc(s["acc_ps"], 1)

            pe.wait_ge(const_in, 32)
            pe.wait_ge(cst, 1)
            units(pe, unit)


def constants():
    import numpy as np

    r, c = np.arange(P)[:, None], np.arange(P)[None, :]
    same = r // SLOTS == c // SLOTS
    tok = lambda n: (n % SLOTS >= HIST) & (n % SLOTS < HIST + 4)
    masks = []
    for tile in range(UNITS):
        batch = tile == TILES
        if batch:
            causal, strict = same & (c >= r), same & (c > r)
            prev, cur = tok(r) & (c > r % SLOTS - HIST), same & tok(r) & tok(c) & (c <= r)
            valid = tok(r)
        else:
            causal, strict = c >= r, c > r
            prev, cur = (c > r) & (tile > 0), c <= r
            valid = r >= 0
        levels = [(r // (2 * b) == c // (2 * b)) & (c % (2 * b) >= b) & (r % (2 * b) < b)
                  for b in (1 << i for i in range(LEVELS))]
        rows = r // SLOTS == np.arange(NB)[None, :]
        swm = np.where(np.concatenate([prev, cur], 1), 0.0, -1e30)
        masks.append(np.concatenate([causal, strict, swm, *levels, valid, rows], 1).astype(np.float32))
    sel = np.zeros((P, P), np.float32)
    for p in range(P):
        b, t = p % 32 // 4, p % 4
        sel[p, SLOTS * b + HIST + t] = 1
    return {"masks": np.stack(masks), "sel": sel, "ident": np.eye(P, dtype=np.float32),
            "iota": np.tile(np.arange(TOPK, dtype=np.float32), (P, 1))}


def layout(i):
    import numpy as np

    a = {k: np.asarray(v) for k, v in i.items()}
    w = a["w_in"]
    QW, VW = H * P, H * P
    CONV = 2 * QW + VW
    off_b = CONV + VW
    off_a = off_b + H
    off_sq = off_a + H
    off_sk = off_sq + QH * HD
    off_sv = off_sk + 2 * HD
    swq = w[:, :, off_sq:off_sk].reshape(L, D, 2, 4, HD).transpose(0, 1, 3, 2, 4).reshape(L, D, 4 * P)
    misc = np.concatenate([w[:, :, off_sk:off_sv + 2 * HD], w[:, :, off_b:off_sq]], 2)

    def blocked(m):
        return m.reshape(L, KC, P, 4, P).transpose(0, 2, 3, 1, 4).reshape(L, P, 4096)

    def columns(m):
        return m.reshape(L, KC, P, -1).transpose(0, 2, 1, 3).reshape(L, P, -1)

    big = [blocked(w[:, :, 512 * n:512 * n + 512]) for n in range(3)] + [blocked(swq), columns(w[:, :, CONV:off_b])]
    big += [columns(a["w_out"][:, :, 512 * n:512 * n + 512]) for n in range(2)]
    big += [blocked(a["peer_wq"][:, :, 512 * n:512 * n + 512]) for n in range(4)]
    xs = np.zeros((UNITS, P, D), np.float32)
    xs[:TILES] = a["x_prompt"].reshape(TILES, P, D)
    xs[TILES].reshape(NB, SLOTS, D)[:, HIST:HIST + 4] = a["x_sample"]
    rows = lambda v: np.broadcast_to(v[:, None, :], (L, P, v.shape[1]))
    off = np.broadcast_to((np.arange(L) * NEXP).astype(np.float32)[:, None, None], (L, P, 1))
    lcon = np.concatenate([rows(a["dn_a_log"]), rows(a["dn_dt_bias"]), rows(a["sw_sinks"]), rows(a["dn_norm_g"]), off], 2)
    ck, cv = a["cache_swa_k"].reshape(L, NB, P, P), a["cache_swa_v"].reshape(L, NB, P, P)
    cache = np.concatenate([ck.transpose(0, 3, 1, 2).reshape(L, P, -1), cv.transpose(0, 2, 1, 3).reshape(L, P, -1)], 2)
    c9 = np.concatenate([a["c_prompt"], a["c_sample"]], 0)
    got = {
        "xs": xs, "cT": c9.T.reshape(KC, P, 9).transpose(1, 0, 2).reshape(P, -1),
        "w_ada": a["w_ada"].reshape(L, KC, P, 12, 512).transpose(0, 3, 2, 1, 4).reshape(L, 12, P, 4096),
        "b_ada": a["b_ada"], "g1n": a["norm1_g"], "g2n": a["norm2_g"], "gfin": a["final_norm_g"],
        "w_big": np.stack(big, 1), "w_misc": columns(misc),
        "keysT": a["peer_keys"].transpose(0, 4, 1, 2, 3).reshape(L, P, -1),
        "state": a["state_delta"].transpose(0, 3, 1, 2, 4), "cache": cache,
        "cache_k": ck, "cache_v": cv,
        "hist": a["state_conv"].reshape(L, NB, HIST, CH, P).transpose(0, 4, 3, 1, 2),
        "cw": a["conv_w"].reshape(L, 4, CH, P).transpose(0, 3, 2, 1), "lcon": lcon,
        "peer_u": a["peer_u"].reshape(L * NEXP, D), "peer_v": a["peer_v"].reshape(L * NEXP, D),
        **constants(),
    }
    return {k: np.ascontiguousarray(v) for k, v in got.items()}


OUTS = {
    "y": (L, UNITS, P, D), "delta_p": (L, P, H, P), "conv_p": (L, P, CH, HIST), "kv_p": (L, P, 2 * P),
    "delta_s": (L, P, NB, H, P), "conv_s": (L, P, CH, NB, HIST), "k_s": (L, NB, P, P), "v_s": (L, NB, P, P),
}
SCRATCH = {"xbuf": ((L + 1, UNITS, P, D), F32), "mod": ((L, 9, 6 * D), F32), "b_idx": ((P, EXPERTS), U32),
           "b_gate": ((P, EXPERTS), F32), "b_h2": ((P, D), F32)}


def kernel(**inputs):
    import numpy as np
    import concourse.bacc as bacc
    from concourse.bass_utils import run_bass_kernel_spmd as run

    nc = bacc.Bacc("TRN2", target_bir_lowering=False, num_devices=1)
    arrays = layout(inputs)
    ins = {k: nc.dram_tensor("in_" + k, v.shape, mybir.dt.from_np(v.dtype), kind="ExternalInput").ap() for k, v in arrays.items()}
    outs = {k: nc.dram_tensor("out_" + k, shape, F32, kind="ExternalOutput").ap() for k, shape in OUTS.items()}
    outs |= {k: nc.dram_tensor("dram_" + k, shape, dt).ap() for k, (shape, dt) in SCRATCH.items()}
    trunk(nc, ins, outs)
    r = run(nc, [{"in_" + k: v for k, v in arrays.items()}], core_ids=[0]).results[0]
    r = {k: r["out_" + k] for k in OUTS}
    y = r["y"][L - 1]
    conv_s = r["conv_s"].transpose(0, 3, 4, 2, 1).reshape(L, NB, HIST, CH * P)
    k_p, v_p = (np.ascontiguousarray(r["kv_p"][:, :, n * P:(n + 1) * P]).reshape(L, 1, P, 2, HD) for n in range(2))
    return (
        y[:TILES].reshape(1, TILES * P, D),
        np.ascontiguousarray(y[TILES].reshape(NB, SLOTS, D)[:, HIST:HIST + 4]),
        np.ascontiguousarray(r["delta_p"].transpose(0, 2, 1, 3)).reshape(L, 1, H, P, P),
        np.ascontiguousarray(r["conv_p"].transpose(0, 3, 2, 1)).reshape(L, 1, HIST, CH * P),
        k_p, v_p,
        np.ascontiguousarray(r["delta_s"].transpose(0, 2, 3, 1, 4)),
        np.ascontiguousarray(conv_s),
        r["k_s"].reshape(L, NB, P, 2, HD), r["v_s"].reshape(L, NB, P, 2, HD),
    )
```

```python
from contextlib import ExitStack

import concourse.bass as bass
from concourse import mybir

F32 = mybir.dt.float32
U32 = mybir.dt.uint32
ALU = mybir.AluOpType
ACT = mybir.ActivationFunctionType
AX = mybir.AxisListType.X

P = 128
L = 2
D = 1024
KC = D // P
TILES = 4
UNITS = TILES + 1
NB, SLOTS = 8, 16
HIST = 3
H = 4
CH = 12
QH, HD = 8, 64
NKEY = 128
PKH = 8
TOPK = 16
NEXP = NKEY * NKEY
EXPERTS = PKH * TOPK
EPS = 1e-6
MISC = 264
LEVELS = 7
G = 4
PG = EXPERTS // G
SG = PG // 4
LG = TILES * PG + SG

CHUNKS = ["mod_a", "conv0", "conv1", "conv2", "swq", "z", "misc", "state", "cache",
          "wo0", "wo1", "mod_b", "wq0", "wq1", "wq2", "wq3", "keys"]
BIG = {"conv0": 0, "conv1": 1, "conv2": 2, "swq": 3, "z": 4, "wo0": 5, "wo1": 6,
       "wq0": 7, "wq1": 8, "wq2": 9, "wq3": 10}

PER_UNIT = dict(
    x_in=16, masks_in=16, x_mid=16, x_stored=16, xp_in=32, idx_taken=1, h_normed=1, hT_ps=2, hT_sb=2, conv_ps=3, uT_sb=1, swq_ps=1, swq_sb=1,
    z_ps=1, z_sb=1, misc_ps=1, misc_sb=1, conv_sum=1, conv_silu=1, tail_kept=1, dt_in=1, gb_act=1,
    qkv_ps=3, qkv_sb=3, qk_normed=1, qkT_ps=2, qkT_sb=2, grow=1, g_ps=1, gcol_sb=1, diff_sb=1,
    decay_sb=1, kk_ps=1, at_sb=1, level_b=LEVELS, u1_ps=LEVELS, u1_sb=LEVELS, xu_ps=LEVELS,
    x_level=LEVELS, ks_ps=1, rhs_sb=1, u_ps=1, u_sb=1, o_ps=1, dn_done=1,
    sc_ps=1, sc_max=1, sc_exp=1, pT_ps=4, pT_sb=4, pv_ps=1, mix_sb=1, kv_kept=1,
    mixT_ps=2, mixT_sb=2, wo_ps=2, h2_sb=1, h2T_ps=2, h2T_sb=2, wq_ps=4, wq_sb=4, keys_ps=4,
    keys_sb=4, square_sb=4, root_sb=4, top_sub=1, top_exp=1, topk_sb=1, acc_ps=1, x_out=1)
AHEAD = dict(x_mid=16, x_stored=16, idx_taken=1, x_out=1, keys_ps=1, wq_ps=1)
SEAMS = dict(norm1=0, conv0=1, conv1=1, conv2=1, swq=1, z=1, misc=1, qkv=1, qk=1, decay=1, kk=1,
             **{f"level{i}": 1 for i in range(LEVELS)}, rhs=1, state=1, scores=1, softmax=0, pv=1, wo=1,
             norm2=1, wq0=1, wq1=0, wq2=1, wq3=1, keys=0, top0=1, top1=1, top2=1, top3=1, top4=1, top5=1)
assert sum(SEAMS.values()) == PG
DVE_STEPS = {"prompt": 61, "batch": 63}
ACT_STEPS = {"prompt": 1, "batch": 2}


def trunk(nc, ins, outs):
    with ExitStack() as ctx:
        def sb(name, shape, dt=F32):
            return ctx.enter_context(nc.sbuf_tensor(name, shape, dt))

        def ps(name, shape):
            return ctx.enter_context(nc.psum_tensor(name, shape, F32))

        def sem(name):
            return ctx.enter_context(nc.semaphore(name))

        W = sb("W", [P, 2, 4096])
        ubuf = sb("ubuf", [P, 2, G, D])
        vbuf = sb("vbuf", [P, 2, G, D])
        x = sb("x", [P, D])
        h = sb("h", [P, D])
        hz = sb("hz", [P, 2 * NB * 144])
        h2 = hz[:, 0:D]
        Z = hz[:, :].rearrange("p (i z) -> p i z", i=2)
        h2p, g2p, xp = sb("h2p", [P, D]), sb("g2p", [P, D]), sb("xp", [P, D])
        hT = sb("hT", [P, KC, P])
        uT = sb("uT", [P, CH, HIST + P])
        qkvT = sb("qkvT", [P, CH, P])
        qkv = sb("qkv", [P, CH, P])
        decay = sb("decay", [P, H, P])
        X, XT, AT = (uT[:, 4 * i:4 * i + 4, HIST:HIST + P] for i in range(3))
        BT = sb("BT", [P, H, P])
        U1 = sb("U1", [P, H, P])
        QK = sb("QK", [P, H, P])
        S = sb("S", [P, H, P])
        z = sb("z", [P, H * P])
        mix = qkvT[:, 0:8, :].rearrange("p j n -> p (j n)")
        swqT = sb("swqT", [P, 4, P])
        kcat = sb("kcat", [P, 2, P])
        kvtok = sb("kvtok", [P, 2, 2 * P])
        J = sb("J", [P, 2, 2048])
        cw = sb("cw", [P, CH, 4])
        hist = BT[:, :, :].rearrange("p h n -> p (h n)")[:, 0:CH * NB * HIST].rearrange("p (c b t) -> p c b t", c=CH, b=NB)
        tails = QK[:, :, :].rearrange("p h n -> p (h n)")[:, 0:CH * NB * HIST].rearrange("p (c b t) -> p c b t", c=CH, b=NB)
        small = sb("small", [P, 256])
        v16 = sb("v16", [P, PKH, 2, TOPK])
        i16 = sb("i16", [P, PKH, 2, TOPK], U32)
        if16 = sb("if16", [P, PKH, 2, TOPK])
        ts16 = sb("ts16", [P, PKH, TOPK])
        pos = sb("pos", [P, PKH, TOPK], U32)
        pi = sb("pi", [P, 2, EXPERTS], U32)
        pf = sb("pf", [P, 2, EXPERTS])
        gate, gatep = sb("gate", [P, EXPERTS]), sb("gatep", [P, EXPERTS])
        idx, idxp = sb("idx", [P, EXPERTS], U32), sb("idxp", [P, EXPERTS], U32)
        idxu = sb("idxu", [P, 2, G], U32)
        idxv = sb("idxv", [P, 2, G], U32)
        a4 = sb("a4", [P, 2, 3, G])
        diag = sb("diag", [P, 2, G, P])
        ident = sb("ident", [P, P])
        zeros = sb("zeros", [P, P])
        ones = sb("ones", [P, P])
        sel = sb("sel", [P, P])
        masks = sb("masks", [P, 2 * P + 2 * P + LEVELS * P + 1 + NB])
        iota = sb("iota", [P, TOPK])
        lcon = sb("lcon", [P, 4 + 4 + 8 + P + 1])

        causal = masks[:, 0:P]
        strict = masks[:, P:2 * P]
        swmask = masks[:, 2 * P:4 * P]
        level = [masks[:, (4 + i) * P:(5 + i) * P] for i in range(LEVELS)]
        valid = masks[:, (4 + LEVELS) * P:(4 + LEVELS) * P + 1]
        rowmask = masks[:, (4 + LEVELS) * P + 1:(4 + LEVELS) * P + 1 + NB]
        a_log, dt_bias, sinks = lcon[:, 0:4], lcon[:, 4:8], lcon[:, 8:16]
        norm_g, idx_off = lcon[:, 16:16 + P], lcon[:, 16 + P:17 + P]

        at_ = [0]

        def sm(n):
            at_[0] += n
            return small[:, at_[0] - n:at_[0]]
        ss, rs = sm(1), sm(1)
        rn, ab, ta, tabs, trel = sm(8), sm(8), sm(4), sm(4), sm(4)
        e4, l4, g4, beta, expa = sm(4), sm(4), sm(4), sm(4), sm(4)
        gcol, egc, be, dl, r4 = sm(4), sm(4), sm(4), sm(4), sm(4)
        cdec, mx, es, rl = sm(32), sm(8), sm(8), sm(8)

        B = [ps(f"B{i}", [P, 512]) for i in range(6)]
        ACC = [ps(f"ACC{i}", [P, 512]) for i in range(2)]

        s = {n: sem(n) for n in PER_UNIT}
        w_in = {c: sem("in_" + c) for c in CHUNKS}
        const_in, cst, sel_in = sem("const_in"), sem("cst"), sem("sel_in")
        layer_in, reset, p_stored = sem("layer_in"), sem("reset"), sem("p_stored")
        hist_in, z_made, z_used = sem("hist_in"), sem("z_made"), sem("z_used")
        fin_in, fin_sq, fin_root, fin_out, fin_stored = (sem("fin_" + n) for n in ("in", "square", "root", "out", "stored"))
        peer_order, fin_order = sem("peer_order"), sem("fin_order")
        sup_ps, sup_sb, s_stored = sem("sup_ps"), sem("sup_sb"), sem("s_stored")
        sup_sb_rows = sem("sup_sb_rows")
        z_clear = sem("z_clear")
        tails_sb, tails_stored = sem("tails_sb"), sem("tails_stored")
        bounce_out, bounce_in, cache_out = sem("bounce_out"), sem("bounce_in"), sem("cache_out")
        x0_in = sem("x0_in")
        dve_order, act_order, pool_order, settled = sem("dve_order"), sem("act_order"), sem("pool_order"), sem("settled")
        u_in = [sem(f"u_in{i}") for i in range(2)]
        v_in = [sem(f"v_in{i}") for i in range(2)]
        dots, gelu_sb, ag_sb, diag_sb, v_acc = sem("dots"), sem("gelu_sb"), sem("ag_sb"), sem("diag_sb"), sem("v_acc")
        c_in, wa_in, ba_in = sem("c_in"), [sem("wa_in0"), sem("wa_in1")], sem("ba_in")
        c_silu, mod_ps, mod_sum, mod_sb, mod_out = sem("c_silu"), sem("mod_ps"), sem("mod_sum"), sem("mod_sb"), sem("mod_out")

        V, A, T = nc.vector, nc.scalar, nc.tensor

        def spread(ap, n):
            return ap.unsqueeze(2).to_broadcast([P, ap.shape[1], n])

        def again(ap, n):
            return ap.unsqueeze(1).to_broadcast([P, n, ap.shape[1]])

        def wslot(chunk):
            return W[:, CHUNKS.index(chunk) % 2, :]

        def blocks(chunk):
            return wslot(chunk).rearrange("p (j k n) -> p j k n", j=4, k=KC)

        def cols(chunk):
            return wslot(chunk).rearrange("p (k n) -> p k n", k=KC)

        misc_w = wslot("misc")[:, 0:KC * MISC].rearrange("p (k n) -> p k n", k=KC)
        keys_w = wslot("keys")[:, 0:2048].rearrange("p (j n) -> p j n", j=16)
        SS = wslot("state").rearrange("p (b h d) -> p b h d", b=NB, h=H)
        KcT = wslot("cache")[:, 0:1024].rearrange("p (b n) -> p b n", b=NB)
        Vc = wslot("cache")[:, 1024:2048].rearrange("p (b n) -> p b n", b=NB)
        sh1, A1 = wslot("mod_a")[:, 0:D], wslot("mod_a")[:, D:2 * D]
        g1, sh2, A2 = (wslot("mod_b")[:, i * D:(i + 1) * D] for i in range(3))
        Zd = [Z[:, i, :].rearrange("p (b k) -> p b k", k=144)[:, :, 0:SLOTS] for i in range(2)]
        Zm = [Z[:, i, 0:NB * P].rearrange("p (b k) -> p b k", b=NB) for i in range(2)]
        sc = J[:, 0, :]
        sc2 = J[:, 1, :]
        PT = J[:, 1, :].rearrange("p (j n) -> p j n", j=16)
        qpT = PT
        ET = U1
        R = BT
        fin = W[:, :, :].rearrange("p i (r d) -> p (i r) d", d=D)
        h3 = lambda ap: ap.rearrange("p (h n) -> p h n", h=H)
        arena = ubuf[:, :, :, :].rearrange("p a g d -> p (a g d)")
        mod9 = arena[0:9, 0:6 * D]
        bada9 = vbuf[0:9, :, :, :].rearrange("p a g d -> p (a g d)")[:, 0:6 * D]
        ng9 = hz[0:9, 0:D]
        ng9b = hz[0:9, D:2 * D]
        cT = small[:, 128:128 + 72]

        block = ctx.enter_context(nc.Block())

        def steps(eng, dense, peer, before=None, after=None):
            def both(kind, layer, tile, peer_kind=None):
                groups = peer(peer_kind, layer, tile - 1, layer * UNITS + tile - 1) if peer_kind else iter(())
                seams = []
                for seam in dense(kind, layer, tile, layer * UNITS + tile):
                    seams.append(seam)
                    for _ in range(SEAMS[seam]):
                        next(groups, None)
                assert seams == list(SEAMS), seams
                for _ in groups:
                    pass

            with eng.Fori(0, L) as layer:
                if before:
                    before(layer)
                both("prompt", layer, 0)
                with eng.Fori(1, TILES) as tile:
                    both("prompt", layer, tile, "prompt")
                if after:
                    after(layer)
                both("batch", layer, TILES, "prompt")
                for _ in peer("batch", layer, TILES, layer * UNITS + TILES):
                    pass

        def waiter(eng, u):
            def wait(name, n):
                eng.wait_ge(s[name], u * PER_UNIT[name] + AHEAD.get(name, 0) + n)
            return wait

        @block.sync
        def _(sp):
            def settle():
                sp.sem_inc(settled, 1)

            sp.dma_start(outs["xbuf"][0], ins["xs"]).then_inc(x0_in, 16)
            sp.dma_start(cT, ins["cT"]).then_inc(c_in, 16)
            sp.dma_start(ident[:], ins["ident"]).then_inc(const_in, 16)
            sp.dma_start(iota[:], ins["iota"]).then_inc(const_in, 16)
            sp.dma_start(sel[:], ins["sel"]).then_inc(sel_in, 16)
            for l in range(L):
                if l:
                    sp.wait_ge(mod_out, 16 * l)
                    settle()
                sp.dma_start(bada9, ins["b_ada"][l].partition_broadcast(9)).then_inc(ba_in, 16)
                sp.dma_start(ng9, ins["g1n"][l].partition_broadcast(9)).then_inc(ba_in, 16)
                sp.dma_start(ng9b, ins["g2n"][l].partition_broadcast(9)).then_inc(ba_in, 16)
                for j in range(12):
                    n = 12 * l + j
                    if n >= 2:
                        sp.wait_ge(mod_ps, n - 1)
                    sp.dma_start(W[:, n % 2, :], ins["w_ada"][l, j]).then_inc(wa_in[n % 2], 16)
                sp.wait_ge(mod_sb, l + 1)
                sp.dma_start(outs["mod"][l], mod9).then_inc(mod_out, 16)
            sp.wait_ge(mod_out, 16 * L)
            sp.wait_ge(x0_in, 16)

            def layer_start(layer):
                sp.wait_ge(s["x_stored"], 16 + 16 * UNITS * layer)
                settle()
                sp.dma_start(lcon[:], ins["lcon"][layer]).then_inc(layer_in, 16)
                sp.dma_start(cw[:], ins["cw"][layer]).then_inc(layer_in, 16)

            def prompt_end(layer):
                last = waiter(sp, layer * UNITS + TILES - 1)
                last("x_mid", 16)
                settle()
                last("tail_kept", 1)
                settle()
                last("kv_kept", 1)
                settle()
                sp.dma_start(outs["delta_p"][layer], S[:]).then_inc(p_stored, 16)
                sp.dma_start(outs["conv_p"][layer], uT[:, :, 0:HIST]).then_inc(p_stored, 16)
                sp.dma_start(outs["kv_p"][layer], kvtok[:, 0, :]).then_inc(p_stored, 16)
                sp.dma_start(hist, ins["hist"][layer]).then_inc(hist_in, 16)

            def dense(kind, layer, tile, u):
                wait = waiter(sp, u)
                batch = kind == "batch"
                wait("x_mid", 0)
                settle()
                sp.dma_start(x[:], outs["xbuf"][layer, tile]).then_inc(s["x_in"], 16)
                sp.dma_start(masks[:], ins["masks"][tile]).then_inc(s["masks_in"], 16)
                freed = dict(mod_a=("h_normed", 1), conv0=("conv_ps", 1), conv1=("conv_ps", 2),
                             conv2=("conv_ps", 3), swq=("swq_ps", 1), z=("z_ps", 1),
                             misc=("misc_ps", 1), wo0=("wo_ps", 1), wo1=("wo_ps", 2),
                             mod_b=("h2_sb", 1), wq0=("wq_ps", 1), wq1=("wq_ps", 2),
                             wq2=("wq_ps", 3), cache=("pv_ps", 1), before0=("keys_ps", 0), before1=("wq_ps", 0))
                last = ["before0", "before1"]
                for c in CHUNKS:
                    i = CHUNKS.index(c) % 2
                    if c in ("state", "cache") and not batch:
                        continue
                    if last[i] == "state":
                        sp.wait_ge(s_stored, 16 * (layer + 1))
                    else:
                        wait(*freed[last[i]])
                    settle()
                    if last[i] == "mod_b":
                        sp.dma_start(outs["xbuf"][layer + 1, tile], x[:]).then_inc(s["x_mid"], 16)
                    last[i] = c
                    if c in BIG:
                        dst, src = wslot(c), ins["w_big"][layer, BIG[c]]
                    elif c == "misc":
                        dst, src = wslot(c)[:, 0:KC * MISC], ins["w_misc"][layer]
                    elif c == "keys":
                        dst, src = wslot(c)[:, 0:2048], ins["keysT"][layer]
                    elif c == "state":
                        dst, src = SS, ins["state"][layer]
                    elif c == "cache":
                        dst, src = wslot(c)[:, 0:2048], ins["cache"][layer]
                    else:
                        rows = (0, 2) if c == "mod_a" else (2, 5)
                        n = (rows[1] - rows[0]) * D
                        dst = wslot(c)[:, 0:n]
                        src = mod_rows(layer, batch, rows[0] * D, n)
                    sp.dma_start(dst, src).then_inc(w_in[c], 16)
                    if c == "state":
                        sp.wait_ge(tails_sb, layer + 1)
                        settle()
                        sp.dma_start(outs["conv_s"][layer], tails).then_inc(tails_stored, 16)
                    if c == "cache":
                        sp.wait_ge(sup_sb, 4 * (layer + 1))
                        settle()
                        sp.dma_start(outs["delta_s"][layer], SS).then_inc(s_stored, 16)
                if batch:
                    for n, cache in enumerate(("k", "v")):
                        sp.dma_start(outs[cache + "_s"][layer, :, 0:P - 4, :],
                                     ins["cache_" + cache][layer, :, 4:P, :]).then_inc(cache_out, 16)
                        for b in range(NB):
                            lo = SLOTS * b + HIST
                            sp.dma_start(outs[cache + "_s"][layer, b, P - 4:P, :],
                                         kvtok[lo:lo + 4, 1, n * P:(n + 1) * P]).then_inc(cache_out, 16)
                    wait("topk_sb", 1)
                    settle()
                    sp.dma_start(outs["b_idx"], idx[:]).then_inc(bounce_out, 16)
                    sp.dma_start(outs["b_gate"], gate[:]).then_inc(bounce_out, 16)
                    sp.dma_start(outs["b_h2"], h2).then_inc(bounce_out, 16)
                    sp.wait_ge(bounce_out, 48 * (layer + 1))
                    settle()
                    EQ = EXPERTS // 4
                    for q in range(4):
                        for b in range(NB):
                            lo = 32 * q + 4 * b
                            r = slice(SLOTS * b + HIST, SLOTS * b + HIST + 4)
                            sp.dma_start(idx[lo:lo + 4, 0:EQ], outs["b_idx"][r, EQ * q:EQ * q + EQ]).then_inc(bounce_in, 16)
                            sp.dma_start(gate[lo:lo + 4, 0:EQ], outs["b_gate"][r, EQ * q:EQ * q + EQ]).then_inc(bounce_in, 16)
                            sp.dma_start(h2[lo:lo + 4, :], outs["b_h2"][r, :]).then_inc(bounce_in, 16)
                yield from SEAMS
                wait("x_out", 0)
                settle()
                wait("x_mid", 16)
                settle()
                wait("x_stored", 0)
                settle()
                sp.dma_start(xp[:], outs["xbuf"][layer + 1, tile]).then_inc(s["xp_in"], 16)
                sp.dma_start(g2p[:], mod_rows(layer, batch, 5 * D, D)).then_inc(s["xp_in"], 16)

            def peer(kind, layer, tile, u):
                wait = waiter(sp, u)
                wait("x_out", 1)
                settle()
                sp.dma_start(outs["xbuf"][layer + 1, tile], xp[:]).then_inc(s["x_stored"], 16)
                if kind == "batch":
                    wait("x_stored", 16)
                    settle()
                yield

            def mod_rows(layer, batch, lo, n):
                m = outs["mod"][layer, :, lo:lo + n]
                if batch:
                    return m[1:9].unsqueeze(1).to_broadcast([NB, SLOTS, n])
                return m[0].partition_broadcast(P)

            steps(sp, dense, peer, layer_start, prompt_end)
            for tile in range(UNITS):
                sp.dma_start(fin[:, tile, :], outs["xbuf"][L, tile]).then_inc(fin_in, 16)
            sp.dma_start(fin[:, UNITS, :], ins["gfin"].partition_broadcast(P)).then_inc(fin_in, 16)
            for tile in range(UNITS):
                sp.wait_ge(fin_out, tile + 1)
                sp.dma_start(outs["y"][tile], fin[:, tile, :]).then_inc(fin_stored, 16)
            sp.wait_ge(fin_stored, 16 * UNITS)
            sp.wait_ge(s["x_stored"], 16 + 16 * L * UNITS)
            sp.wait_ge(p_stored, 48 + 48 * L)
            sp.wait_ge(s_stored, 16 * L)
            sp.wait_ge(tails_stored, 16 + 16 * L)
            sp.wait_ge(cache_out, 16 * 18 * (L + 1))
            sp.wait_ge(bounce_in, 16 * 96 * L)

        @block.gpsimd
        def _(pool):
            g = nc.gpsimd
            g.memset(zeros[:], 0.0)
            g.memset(ones[:], 1.0).then_inc(cst, 1)
            pool.wait_ge(cst, 1)

            def settle():
                pool.sem_inc(settled, 1)

            def layer_start(layer):
                pool.wait_ge(p_stored, 48 + 48 * layer)
                pool.wait_ge(s["x_stored"], 16 + 16 * UNITS * layer)
                settle()
                g.tensor_copy(uT[:, :, 0:HIST], zeros[:, 0:CH * HIST].rearrange("p (c t) -> p c t", c=CH))
                g.tensor_copy(kcat[:, 0, :], zeros[:])
                g.tensor_copy(kvtok[:, 0, 0:P], zeros[:])
                g.tensor_copy(kvtok[:, 0, P:2 * P], zeros[:])
                for hh in range(H):
                    last = g.tensor_copy(S[:, hh, :], zeros[:])
                last.then_inc(reset, 1)

            def dense(kind, layer, tile, u):
                yield from SEAMS

            def peer(kind, layer, tile, u):
                wait = waiter(pool, u)
                batch = kind == "batch"
                if batch:
                    pool.wait_ge(bounce_in, 16 * 96 * (layer + 1))
                else:
                    wait("topk_sb", 1)
                settle()
                g.tensor_copy(idxp[:], idx[:]).then_inc(s["idx_taken"], 1)
                wait("idx_taken", 1)
                settle()
                groups = SG if batch else PG
                first = layer * LG + tile * PG
                with pool.Fori(0, groups // 2) as i:
                    for par in range(2):
                        n = first + i * 2 + par
                        pool.wait_ge(dots, n + 1)
                        settle()
                        now = idxp[:, bass.ds(i * (2 * G) + par * G, G)]
                        g.tensor_copy(idxu[:, par, :], now).then_inc(pool_order, 1)
                        pool.wait_ge(pool_order, n * 2 + 1)
                        settle()
                        for j in range(G):
                            off = bass.IndirectOffsetOnAxis(ap=idxu[:, par, j:j + 1], axis=0)
                            g.indirect_dma_start(out=ubuf[:, par, j, :], out_offset=None, in_=ins["peer_u"],
                                                 in_offset=off).then_inc(u_in[par], 16)
                        pool.wait_ge(v_acc, n + 1)
                        settle()
                        g.tensor_copy(idxv[:, par, :], now).then_inc(pool_order, 1)
                        pool.wait_ge(pool_order, n * 2 + 2)
                        settle()
                        for j in range(G):
                            off = bass.IndirectOffsetOnAxis(ap=idxv[:, par, j:j + 1], axis=0)
                            g.indirect_dma_start(out=vbuf[:, par, j, :], out_offset=None, in_=ins["peer_v"],
                                                 in_offset=off).then_inc(v_in[par], 16)
                yield

            steps(pool, dense, peer, layer_start)

        @block.scalar
        def _(act):
            state = {"base": 0, "n": 0}

            def link(instruction):
                state["n"] += 1
                instruction.then_inc(act_order, 1)
                act.wait_ge(act_order, state["base"] + state["n"])

            act.wait_ge(c_in, 16)
            A.activation(cT, cT, ACT.Silu).then_inc(c_silu, 1)

            def four(bank):
                return bank[:].rearrange("p (j n) -> p j n", j=4)

            def dense(kind, layer, tile, u):
                wait = waiter(act, u)
                batch = kind == "batch"
                a, b = ACT_STEPS["prompt"], ACT_STEPS["batch"]
                state["base"] = layer * (TILES * a + b) + tile * a
                state["n"] = 0
                nx = [0]

                def root(nth, ap):
                    wait("square_sb", nth)
                    A.activation(ap, ap, ACT.Sqrt).then_inc(s["root_sb"], 1)

                def expand(src):
                    n = nx[0]
                    if n >= 2:
                        act.wait_ge(z_used, 20 * layer + n - 1)
                    A.copy(Zd[n % 2], src.rearrange("p (b t) -> p b t", b=NB)).then_inc(z_made, 1)
                    nx[0] += 1

                def channels(i):
                    wait("conv_ps", i + 1)
                    return A.copy(uT[:, 4 * i:4 * i + 4, HIST:HIST + P], four(B[2 + i]))

                root(1, ss)
                for i in range(2):
                    wait("hT_ps", i + 1)
                    A.copy(hT[:, 4 * i:4 * i + 4, :], four(B[i])).then_inc(s["hT_sb"], 1)
                yield "norm1"
                yield "conv0"
                if not batch:
                    act.wait_ge(reset, layer + 1)
                channels(0)
                yield "conv1"
                channels(1)
                yield "conv2"
                last = channels(2)
                if batch:
                    act.wait_ge(hist_in, 16 * (layer + 1))
                    link(last)
                    dst = uT[:, :, HIST:HIST + P].rearrange("p c (b t) -> p c b t", b=NB)[:, :, :, 0:HIST]
                    last = A.copy(dst, hist)
                last.then_inc(s["uT_sb"], 1)
                yield "swq"
                wait("swq_ps", 1)
                A.mul(swqT[:], four(B[5]), HD ** -0.5).then_inc(s["swq_sb"], 1)
                yield "z"
                wait("z_ps", 1)
                A.activation(z[:], B[0][:], ACT.Silu).then_inc(s["z_sb"], 1)
                if batch:
                    src = uT[:, :, HIST:HIST + P].rearrange("p c (b t) -> p c b t", b=NB)
                    A.copy(tails, src[:, :, :, HIST + 1:HIST + 4]).then_inc(tails_sb, 1)
                wait("conv_sum", 1)
                A.copy(uT[:, :, 0:HIST], uT[:, :, P:P + HIST]).then_inc(s["tail_kept"], 1)
                A.activation(qkvT[:], qkvT[:], ACT.Silu).then_inc(s["conv_silu"], 1)
                yield "misc"
                wait("misc_ps", 1)
                act.wait_ge(cache_out, 16 * 18 * (layer + 1))
                A.copy(kcat[:, 1, :], B[1][:, MISC:MISC + P])
                A.copy(kvtok[:, 1, :], B[1][:, 0:2 * P])
                A.copy(ab, B[1][:, 2 * P:MISC]).then_inc(s["misc_sb"], 1)
                wait("dt_in", 1)
                link(A.activation(e4, tabs, ACT.Exp, scale=-1.0))
                A.activation(expa, a_log, ACT.Exp)
                A.activation(l4, e4, ACT.Ln, bias=1.0)
                A.activation(beta, ab[:, 0:4], ACT.Sigmoid).then_inc(s["gb_act"], 1)
                for i in range(3):
                    wait("qkv_ps", i + 1)
                    A.copy(qkv[:, 4 * i:4 * i + 4, :], four(B[2 + i])).then_inc(s["qkv_sb"], 1)
                yield "qkv"
                root(2, rn)
                for i in range(2):
                    wait("qkT_ps", i + 1)
                    A.copy(qkvT[:, 4 * i:4 * i + 4, :], four(B[i])).then_inc(s["qkT_sb"], 1)
                yield "qk"
                wait("g_ps", 1)
                A.copy(gcol, B[5][:, 0:4])
                A.activation(egc, B[5][:, 0:4], ACT.Exp)
                if batch:
                    ends = B[2][:].rearrange("p (g t) -> p g t", t=SLOTS)[:, :, SLOTS - 1]
                    last = A.activation(cdec, ends, ACT.Exp)
                else:
                    last = A.activation(cdec[:, 0:H], h3(B[2][:])[:, :, P - 1], ACT.Exp)
                last.then_inc(s["gcol_sb"], 1)
                wait("diff_sb", 1)
                A.activation(decay[:], decay[:], ACT.Exp).then_inc(s["decay_sb"], 1)
                yield "decay"
                yield "kk"
                for i in range(LEVELS):
                    wait("u1_ps", i + 1)
                    A.copy(U1[:], h3(B[0][:])).then_inc(s["u1_sb"], 1)
                    yield f"level{i}"
                if batch:
                    act.wait_ge(z_clear, layer + 1)
                    for j in (4, 5, 6, 7, 0, 1, 2, 3):
                        expand(qkvT[:, j, :])
                wait("u_ps", 1)
                A.copy(ET[:], h3(B[0][:])).then_inc(s["u_sb"], 1)
                yield "rhs"
                root(3, r4)
                yield "state"
                if batch:
                    for hb in range(4):
                        expand(swqT[:, hb, :])
                yield "scores"
                wait("sc_max", 1)
                A.activation(sc, sc, ACT.Exp)
                A.activation(es, es, ACT.Exp).then_inc(s["sc_exp"], 1)
                yield "softmax"
                for i in range(4):
                    wait("pT_ps", i + 1)
                    A.copy(PT[:, 4 * i:4 * i + 4, :], four(B[(4, 5, 0, 1)[i]])).then_inc(s["pT_sb"], 1)
                    if batch:
                        wait("pT_sb", i + 1)
                        expand(PT[:, 4 * i, :])
                        expand(PT[:, 4 * i + 2, :])
                yield "pv"
                wait("pv_ps", 1)
                A.copy(kcat[:, 0, :], kcat[:, 1, :])
                A.copy(kvtok[:, 0, :], kvtok[:, 1, :]).then_inc(s["kv_kept"], 1)
                for i in range(2):
                    wait("mixT_ps", i + 1)
                    A.copy(hT[:, 4 * i:4 * i + 4, :], four(B[3 + i])).then_inc(s["mixT_sb"], 1)
                yield "wo"
                root(4, ss)
                for i in range(2):
                    wait("h2T_ps", i + 1)
                    A.copy(hT[:, 4 * i:4 * i + 4, :], four(B[2 + i])).then_inc(s["h2T_sb"], 1)
                yield "norm2"
                for i in range(4):
                    yield f"wq{i}"
                    wait("wq_ps", i + 1)
                    A.copy(qpT[:, 4 * i:4 * i + 4, :], four(B[(4, 5, 0, 1)[i]])).then_inc(s["wq_sb"], 1)
                yield "keys"
                for i in range(4):
                    wait("keys_ps", i + 1)
                    A.copy(sc[:, 512 * i:512 * i + 512], B[2 + i][:]).then_inc(s["keys_sb"], 1)
                for i in range(5):
                    yield f"top{i}"
                wait("top_sub", 1)
                A.activation(gate[:], gate[:], ACT.Exp).then_inc(s["top_exp"], 1)
                yield "top5"
                assert state["n"] == ACT_STEPS[kind], ("ACT", kind, state["n"])

            def peer(kind, layer, tile, u):
                batch = kind == "batch"
                first = layer * LG + tile * PG
                pick = sel if batch else ident

                def diagonals(k):
                    act.wait_ge(ag_sb, first + k + 1)
                    act.wait_ge(v_acc, first + k + 1)
                    for j in range(G):
                        last = A.activation(diag[:, k % 2, j, :], pick[:], ACT.Copy, scale=a4[:, k % 2, 2, j:j + 1])
                    last.then_inc(diag_sb, 1)
                groups = SG if batch else PG
                for k in range(groups):
                    if k:
                        diagonals(k - 1)
                    act.wait_ge(dots, first + k + 3)
                    A.activation(a4[:, k % 2, 1, :], a4[:, k % 2, 0, :], ACT.Gelu).then_inc(gelu_sb, 1)
                    yield
                diagonals(groups - 1)

            act.wait_ge(const_in, 32)
            act.wait_ge(sel_in, 16)
            steps(act, dense, peer)
            for tile in range(UNITS):
                act.wait_ge(fin_sq, tile + 1)
                A.activation(ss, ss, ACT.Sqrt).then_inc(fin_root, 1)

        @block.vector
        def _(dve):
            state = {"base": 0, "n": 0}

            def link(instruction):
                state["n"] += 1
                instruction.then_inc(dve_order, 1)
                dve.wait_ge(dve_order, state["base"] + state["n"])

            def settle():
                dve.sem_inc(settled, 1)

            dve.sem_inc(dots, 2)
            dve.sem_inc(v_acc, 2)
            for name, n in AHEAD.items():
                dve.sem_inc(s[name], n)
            dve.sem_inc(p_stored, 48)
            dve.sem_inc(tails_stored, 16)
            dve.sem_inc(cache_out, 16 * 18)
            for l in range(L):
                dve.wait_ge(ba_in, 48 * (l + 1))
                for j in range(12):
                    dve.wait_ge(mod_ps, 12 * l + j + 1)
                    last = V.tensor_tensor(mod9[:, 512 * j:512 * j + 512], B[j % 2][0:9, :],
                                           bada9[:, 512 * j:512 * j + 512], ALU.add)
                    if j < 11:
                        last.then_inc(mod_sum, 1)
                last.then_inc(mod_sum, 1)
                dve.wait_ge(mod_sum, 12 * (l + 1))
                m = mod9
                V.scalar_tensor_tensor(m[:, D:2 * D], m[:, D:2 * D], 1.0, ng9, ALU.add, ALU.mult)
                V.scalar_tensor_tensor(m[:, 4 * D:5 * D], m[:, 4 * D:5 * D], 1.0, ng9b, ALU.add, ALU.mult).then_inc(mod_sb, 1)

            def norm(wait, nth, src, out, gain, shift):
                link(V.tensor_tensor_reduce(out, src, src, 1.0, 0.0, ALU.mult, ALU.add, ss))
                V.tensor_scalar(ss, ss, 1.0 / D, EPS, ALU.mult, ALU.add).then_inc(s["square_sb"], 1)
                wait("root_sb", nth)
                link(V.reciprocal(rs, ss))
                last = V.scalar_tensor_tensor(out, src, rs, gain, ALU.mult, ALU.mult)
                if shift is not None:
                    link(last)
                    last = V.tensor_tensor(out, out, shift, ALU.add)
                return last

            def dense(kind, layer, tile, u):
                wait = waiter(dve, u)
                batch = kind == "batch"
                a, b = DVE_STEPS["prompt"], DVE_STEPS["batch"]
                state["base"] = layer * (TILES * a + b) + tile * a
                state["n"] = 0
                wait("x_in", 16)
                dve.wait_ge(w_in["mod_a"], 16 * (u + 1))
                norm(wait, 1, x[:], h[:], A1, sh1).then_inc(s["h_normed"], 1)
                yield "norm1"
                yield "conv0"
                if batch:
                    V.memset(hz[:], 0.0).then_inc(z_clear, 1)
                yield "conv1"
                yield "conv2"
                wait("uT_sb", 1)
                dve.wait_ge(reset, layer + 1)
                dve.wait_ge(layer_in, 32 * (layer + 1))
                wait("masks_in", 16)
                tmp = sc[:, 0:CH * P].rearrange("p (c t) -> p c t", c=CH)
                link(V.tensor_tensor(qkvT[:], uT[:, :, 0:P], spread(cw[:, :, 0], P), ALU.mult))
                for i in range(1, 4):
                    link(V.tensor_tensor(tmp, uT[:, :, i:i + P], spread(cw[:, :, i], P), ALU.mult))
                    last = V.tensor_tensor(qkvT[:], qkvT[:], tmp, ALU.add)
                    if i < 3:
                        link(last)
                    if i == 1:
                        yield "swq"
                last.then_inc(s["conv_sum"], 1)
                yield "z"
                yield "misc"
                wait("misc_sb", 1)
                link(V.tensor_tensor(ta, ab[:, 4:8], dt_bias, ALU.add))
                V.tensor_scalar(trel, ta, 0.0, None, ALU.max)
                V.scalar_tensor_tensor(tabs, ta, -1.0, ta, ALU.mult, ALU.max).then_inc(s["dt_in"], 1)
                wait("gb_act", 1)
                link(V.tensor_tensor(g4, l4, trel, ALU.add))
                link(V.scalar_tensor_tensor(g4, g4, -1.0, expa, ALU.mult, ALU.mult))
                V.tensor_scalar(g4, g4, valid, None, ALU.mult)
                link(V.tensor_scalar(beta, beta, valid, None, ALU.mult))
                wait("tail_kept", 1)
                for hh in range(H):
                    V.tensor_scalar(X[:, hh, :], causal, g4[:, hh:hh + 1], None, ALU.mult)
                    last = V.tensor_scalar(XT[:, hh, :], ident[:], beta[:, hh:hh + 1], None, ALU.mult)
                last.then_inc(s["grow"], 1)
                yield "qkv"
                wait("qkv_sb", 3)
                qk = qkv[:, 0:8, :]
                sq = sc[:, 0:8 * P].rearrange("p (c t) -> p c t", c=8)
                link(V.tensor_tensor(sq, qk, qk, ALU.mult))
                link(V.tensor_reduce(rn, sq, AX, ALU.add))
                V.tensor_scalar(rn, rn, EPS, None, ALU.add).then_inc(s["square_sb"], 1)
                wait("root_sb", 2)
                link(V.reciprocal(rn, rn))
                link(V.tensor_scalar(rn[:, 0:4], rn[:, 0:4], P ** -0.5, None, ALU.mult))
                V.tensor_tensor(qk, qk, spread(rn, P), ALU.mult).then_inc(s["qk_normed"], 1)
                yield "qk"
                wait("g_ps", 1)
                wait("gcol_sb", 1)
                for hh in range(H):
                    last = V.tensor_scalar(decay[:, hh, :], h3(B[2][:])[:, hh, :], gcol[:, hh:hh + 1], 0.0, ALU.subtract, ALU.min)
                last.then_inc(s["diff_sb"], 1)
                wait("decay_sb", 1)
                link(V.tensor_tensor(decay[:], decay[:], again(causal, H), ALU.mult))
                yield "decay"
                wait("kk_ps", 1)
                link(V.tensor_tensor(AT, h3(B[4][:]), decay[:], ALU.mult))
                link(V.tensor_tensor(AT, AT, again(strict, H), ALU.mult))
                link(V.tensor_tensor(AT, AT, h3(B[3][:]), ALU.mult))
                if batch:
                    dve.wait_ge(tails_stored, 16 + 16 * (layer + 1))
                V.tensor_tensor(QK[:], h3(B[1][:]), decay[:], ALU.mult)
                V.tensor_tensor(qkv[:, 8:12, :], qkv[:, 8:12, :], spread(beta, P), ALU.mult)
                V.scalar_tensor_tensor(be, beta, -1.0, egc, ALU.mult, ALU.mult)
                V.tensor_copy(X, again(ident[:], H))
                V.tensor_copy(XT, again(ident[:], H))
                if batch:
                    ends = decay[:].rearrange("p h (b t) -> p h b t", t=SLOTS)[:, :, :, SLOTS - 1]
                    link(V.tensor_reduce(dl, ends, AX, ALU.add))
                else:
                    link(V.tensor_copy(dl, decay[:, :, P - 1]))
                wait("qkT_sb", 2)
                V.tensor_tensor(qkv[:, 4:8, :], qkv[:, 4:8, :], spread(dl, P), ALU.mult).then_inc(s["at_sb"], 1)
                yield "kk"
                for i in range(LEVELS):
                    V.tensor_tensor(BT[:], AT, again(level[i], H), ALU.mult).then_inc(s["level_b"], 1)
                    wait("xu_ps", i + 1)
                    V.tensor_tensor(X, X, h3(B[2][:]), ALU.subtract)
                    V.tensor_tensor(XT, XT, h3(B[3][:]), ALU.subtract).then_inc(s["x_level"], 1)
                    wait("x_level", i + 1)
                    yield f"level{i}"
                wait("ks_ps", 1)
                link(V.tensor_tensor(R[:], h3(B[4][:]), spread(be, P), ALU.mult))
                V.tensor_tensor(R[:], R[:], qkv[:, 8:12, :], ALU.add).then_inc(s["rhs_sb"], 1)
                yield "rhs"
                od = h3(mix[:, 0:H * P])
                link(V.tensor_tensor(od, h3(B[5][:]), spread(egc, P), ALU.mult))
                wait("o_ps", 1)
                link(V.tensor_tensor(od, od, h3(B[1][:]), ALU.add))
                if batch:
                    dve.wait_ge(w_in["state"], 16 * (layer + 1))
                    for hh in range(H):
                        if hh >= 2:
                            dve.wait_ge(sup_ps, 4 * layer + hh - 1)
                        kd = sc2 if hh % 2 else sc
                        V.tensor_tensor(kd[:, 0:NB * P].rearrange("p (b d) -> p b d", b=NB),
                                        again(qkv[:, 4 + hh, :], NB), spread(rowmask, P), ALU.mult).then_inc(sup_sb_rows, 1)
                        link(V.tensor_tensor(SS[:, :, hh, :], SS[:, :, hh, :], spread(cdec[:, NB * hh:NB * hh + NB], P), ALU.mult))
                        dve.wait_ge(sup_ps, 4 * layer + hh + 1)
                        V.tensor_tensor(SS[:, 0:4, hh, :], SS[:, 0:4, hh, :], h3(B[2][:]), ALU.add)
                        V.tensor_tensor(SS[:, 4:8, hh, :], SS[:, 4:8, hh, :], h3(B[3][:]), ALU.add).then_inc(sup_sb, 1)
                    last = None
                else:
                    link(V.tensor_tensor(S[:], S[:], spread(cdec[:, 0:H], P), ALU.mult))
                    link(V.tensor_tensor(S[:], S[:], h3(B[2][:]), ALU.add))
                yield "state"
                wait("z_sb", 1)
                sq = sc[:, 0:H * P].rearrange("p (c t) -> p c t", c=H)
                if batch:
                    dve.wait_ge(sup_ps, 4 * layer + 4)
                link(V.tensor_tensor(sq, od, od, ALU.mult))
                link(V.tensor_reduce(r4, sq, AX, ALU.add))
                V.tensor_scalar(r4, r4, 1.0 / P, EPS, ALU.mult, ALU.add).then_inc(s["square_sb"], 1)
                wait("root_sb", 3)
                link(V.reciprocal(r4, r4))
                link(V.tensor_tensor(od, od, spread(r4, P), ALU.mult))
                link(V.tensor_tensor(od, od, again(norm_g, H), ALU.mult))
                V.tensor_tensor(mix[:, 0:H * P], mix[:, 0:H * P], z[:], ALU.mult).then_inc(s["dn_done"], 1)
                wait("sc_ps", 1)
                for i in range(4):
                    last = V.tensor_tensor(sc[:, 512 * i:512 * i + 512].rearrange("p (h k) -> p h k", h=2),
                                           B[i][:].rearrange("p (h k) -> p h k", h=2), again(swmask, 2), ALU.add)
                link(last)
                sc3 = sc.rearrange("p (h k) -> p h k", h=QH)
                link(V.tensor_reduce(mx, sc3, AX, ALU.max))
                link(V.tensor_tensor(mx, mx, sinks, ALU.max))
                V.tensor_tensor(es, sinks, mx, ALU.subtract)
                V.tensor_tensor(sc3, sc3, spread(mx, 2 * P), ALU.subtract).then_inc(s["sc_max"], 1)
                yield "scores"
                wait("sc_exp", 1)
                link(V.tensor_reduce(rl, sc3, AX, ALU.add))
                link(V.tensor_tensor(rl, rl, es, ALU.add))
                link(V.reciprocal(rl, rl))
                yield "softmax"
                wait("pv_ps", 1)
                V.tensor_tensor(mix[:, H * P:].rearrange("p (h d) -> p h d", h=QH),
                                B[2][:].rearrange("p (h d) -> p h d", h=QH), spread(rl, HD), ALU.mult).then_inc(s["mix_sb"], 1)
                yield "pv"
                yield "wo"
                wait("wo_ps", 2)
                dve.wait_ge(w_in["mod_b"], 16 * (u + 1))
                for i in range(2):
                    last = V.tensor_tensor(h[:, 512 * i:512 * i + 512], B[i][:], g1[:, 512 * i:512 * i + 512], ALU.mult)
                link(last)
                link(V.tensor_tensor(x[:], x[:], h[:], ALU.add))
                norm(wait, 4, x[:], h2, A2, sh2).then_inc(s["h2_sb"], 1)
                for c in ("norm2", "wq0", "wq1", "wq2", "wq3", "keys"):
                    yield c
                wait("keys_sb", 4)

                def best16(src, spare, vals, idxs, rows, n, seam):
                    row = lambda ap, j: ap[:, n * j:n * j + n]
                    settle()
                    for j in range(rows):
                        last = V.max(vals[:, j, 0:8], row(src, j))
                    link(last)
                    settle()
                    for j in range(rows):
                        V.max_index(idxs[:, j, 0:8], vals[:, j, 0:8], row(src, j))
                        last = V.match_replace(row(spare, j), vals[:, j, 0:8], row(src, j), -3e38)
                    link(last)
                    settle()
                    yield seam
                    for j in range(rows):
                        last = V.max(vals[:, j, 8:16], row(spare, j))
                    link(last)
                    settle()
                    for j in range(rows):
                        last = V.max_index(idxs[:, j, 8:16], vals[:, j, 8:16], row(spare, j))
                    link(last)
                yield from best16(sc, sc2, v16[:].rearrange("p h s k -> p (h s) k"), i16[:].rearrange("p h s k -> p (h s) k"), 16, P, "top0")
                yield "top1"
                sums = sc.rearrange("p (h i j) -> p h i j", h=PKH, i=TOPK)
                V.tensor_copy(if16[:], i16[:])
                for hh in range(PKH):
                    last = V.tensor_tensor(sums[:, hh], spread(v16[:, hh, 0, :], TOPK), again(v16[:, hh, 1, :], TOPK), ALU.add)
                link(last)
                yield "top2"
                yield from best16(sc, sc2, ts16[:], pos[:], PKH, TOPK * TOPK, "top3")
                yield "top4"
                V.tensor_tensor(gate[:].rearrange("p (h k) -> p h k", h=PKH), ts16[:],
                                spread(ts16[:, :, 0], TOPK), ALU.subtract).then_inc(s["top_sub"], 1)
                posf = pos[:].rearrange("p h k -> p (h k)")
                V.tensor_scalar(pi[:, 0, :], posf, 4, None, ALU.logical_shift_right)
                link(V.tensor_scalar(pi[:, 1, :], posf, 15, None, ALU.bitwise_and))
                link(V.tensor_copy(pf[:], pi[:]))
                hot = [sc.rearrange("p (k j) -> p k j", j=TOPK), sc2.rearrange("p (k j) -> p k j", j=TOPK)]
                for i in range(2):
                    last = V.tensor_tensor(hot[i], spread(pf[:, i, :], TOPK), again(iota[:], EXPERTS), ALU.is_equal)
                link(last)
                for i in range(2):
                    for hh in range(PKH):
                        k = slice(TOPK * hh, TOPK * hh + TOPK)
                        last = V.tensor_tensor(hot[i][:, k, :], hot[i][:, k, :], again(if16[:, hh, i, :], TOPK), ALU.mult)
                link(last)
                for i in range(2):
                    last = V.tensor_reduce(pf[:, i, :], hot[i], AX, ALU.add)
                link(last)
                link(V.scalar_tensor_tensor(pf[:, 0, :], pf[:, 0, :], float(NKEY), pf[:, 1, :], ALU.mult, ALU.add))
                link(V.tensor_scalar(pf[:, 0, :], pf[:, 0, :], idx_off, None, ALU.add))
                wait("idx_taken", 0)
                V.tensor_copy(idx[:], pf[:, 0, :])
                wait("top_exp", 1)
                g3 = gate[:].rearrange("p (h k) -> p h k", h=PKH)
                link(V.tensor_reduce(rn, g3, AX, ALU.add))
                link(V.reciprocal(rn, rn))
                V.tensor_tensor(g3, g3, spread(rn, TOPK), ALU.mult).then_inc(s["topk_sb"], 1)
                assert state["n"] == DVE_STEPS[kind], ("DVE", kind, state["n"])
                yield "top5"

            def peer(kind, layer, tile, u):
                wait = waiter(dve, u)
                batch = kind == "batch"
                first = layer * LG + tile * PG
                half = layer * (LG // 2) + tile * (PG // 2)
                if batch:
                    dve.wait_ge(bounce_in, 16 * 96 * (layer + 1))
                wait("topk_sb", 1)
                wait("x_out", 0)
                V.tensor_copy(h2p[:], h2)
                V.tensor_copy(gatep[:], gate[:]).then_inc(peer_order, 1)
                dve.wait_ge(peer_order, 2 * u + 1)

                def gated(k):
                    dve.wait_ge(gelu_sb, first + k + 1)
                    V.tensor_tensor(a4[:, k % 2, 2, :], a4[:, k % 2, 1, :], gatep[:, G * k:G * k + G],
                                    ALU.mult).then_inc(ag_sb, 1)
                groups = SG if batch else PG
                for k in range(groups):
                    if k:
                        gated(k - 1)
                    dve.wait_ge(u_in[k % 2], (half + k // 2 + 1) * (16 * G))
                    for j in range(G):
                        last = V.tensor_tensor_reduce(ubuf[:, k % 2, j, :], ubuf[:, k % 2, j, :], h2p[:], 1.0, 0.0,
                                                      ALU.mult, ALU.add, a4[:, k % 2, 0, j:j + 1])
                    last.then_inc(dots, 1)
                    yield
                gated(groups - 1)
                wait("acc_ps", 1)
                wait("xp_in", 32)
                for i in range(2):
                    last = V.tensor_tensor(h2p[:, 512 * i:512 * i + 512], ACC[i][:], g2p[:, 512 * i:512 * i + 512], ALU.mult)
                last.then_inc(peer_order, 1)
                dve.wait_ge(peer_order, 2 * u + 2)
                V.tensor_tensor(xp[:], xp[:], h2p[:], ALU.add).then_inc(s["x_out"], 1)

            dve.wait_ge(const_in, 32)
            steps(dve, dense, peer)
            dve.wait_ge(fin_in, 16 * (UNITS + 1))
            for tile in range(UNITS):
                def chain(instruction):
                    instruction.then_inc(fin_order, 1)
                    dve.wait_ge(fin_order, chain.n + 1)
                    chain.n += 1
                chain.n = 3 * tile
                row = fin[:, tile, :]
                chain(V.tensor_tensor_reduce(h[:], row, row, 1.0, 0.0, ALU.mult, ALU.add, ss))
                V.tensor_scalar(ss, ss, 1.0 / D, EPS, ALU.mult, ALU.add).then_inc(fin_sq, 1)
                dve.wait_ge(fin_root, tile + 1)
                chain(V.reciprocal(rs, ss))
                chain(V.scalar_tensor_tensor(row, row, rs, fin[:, UNITS, :], ALU.mult, ALU.mult))
                dve.sem_inc(fin_out, 1)

        @block.tensor
        def _(pe):
            pe.wait_ge(c_silu, 1)
            cT3 = cT.rearrange("p (k c) -> p k c", k=KC)
            for n in range(12 * L):
                pe.wait_ge(wa_in[n % 2], 16 * (n // 2 + 1))
                if n >= 2:
                    pe.wait_ge(mod_sum, n - 1)
                w = W[:, n % 2, :].rearrange("p (k n) -> p k n", k=KC)
                for k in range(KC):
                    last = T.matmul(B[n % 2][0:9, :], cT3[:, k, :], w[:, k, :], start=(k == 0), stop=(k == KC - 1))
                last.then_inc(mod_ps, 1)

            def turn(src, banks, name, wait_for):
                for i, bank in enumerate(banks):
                    wait_for(i)
                    for j in range(4):
                        last = T.transpose(bank[:, P * j:P * j + P], src(4 * i + j), ident[:])
                    last.then_inc(s[name], 1)

            def dense(kind, layer, tile, u):
                wait = waiter(pe, u)
                batch = kind == "batch"
                nz = [0]
                none = lambda i: None

                def chunk(c):
                    n = layer + 1 if c in ("state", "cache") else u + 1
                    pe.wait_ge(w_in[c], 16 * n)

                def expanded(out, rhs, start, stop, done=True):
                    n = nz[0]
                    pe.wait_ge(z_made, 20 * layer + n + 1)
                    for b in range(NB):
                        last = T.matmul(out, Zm[n % 2][:, b, :], rhs(b), start=start and b == 0, stop=stop and b == NB - 1)
                    last.then_inc(z_used, 1)
                    nz[0] += 1

                wait("h_normed", 1)
                turn(lambda j: h[:, P * j:P * j + P], B[0:2], "hT_ps", none)
                yield "norm1"
                wait("hT_sb", 2)
                for i, c in enumerate(("conv0", "conv1", "conv2", "swq")):
                    chunk(c)
                    for j in range(4):
                        for k in range(KC):
                            last = T.matmul(B[2 + i][:, P * j:P * j + P], blocks(c)[:, j, k, :], hT[:, k, :],
                                            start=(k == 0), stop=(k == KC - 1))
                    last.then_inc(s["conv_ps" if i < 3 else "swq_ps"], 1)
                    yield c
                chunk("z")
                for k in range(KC):
                    last = T.matmul(B[0][:], hT[:, k, :], cols("z")[:, k, :], start=(k == 0), stop=(k == KC - 1))
                last.then_inc(s["z_ps"], 1)
                yield "z"
                chunk("misc")
                for k in range(KC):
                    T.matmul(B[1][:, 0:MISC], hT[:, k, :], misc_w[:, k, :], start=(k == 0), stop=(k == KC - 1))
                for k in range(KC):
                    last = T.matmul(B[1][:, MISC:MISC + P], misc_w[:, k, 0:P], hT[:, k, :], start=(k == 0), stop=(k == KC - 1))
                last.then_inc(s["misc_ps"], 1)
                yield "misc"
                wait("conv_silu", 1)
                turn(lambda j: qkvT[:, j, :], B[2:5], "qkv_ps", none)
                yield "qkv"
                wait("qk_normed", 1)
                wait("z_sb", 1)
                wait("misc_sb", 1)
                turn(lambda j: qkv[:, j, :], B[0:2], "qkT_ps", none)
                wait("grow", 1)
                wait("qkv_sb", 3)
                wait("swq_sb", 1)
                T.matmul(h3(B[2][:]), ones[:], X, start=True, stop=True)
                T.matmul(B[5][:, 0:4], causal, g4, start=True, stop=True)
                T.matmul(h3(B[3][:]), ones[:], XT, start=True, stop=True).then_inc(s["g_ps"], 1)
                yield "qk"
                wait("qkT_sb", 2)
                for hh in range(H):
                    T.matmul(B[4][:, P * hh:P * hh + P], qkvT[:, 4 + hh, :], qkvT[:, 4 + hh, :], start=True, stop=True)
                for hh in range(H):
                    last = T.matmul(B[1][:, P * hh:P * hh + P], qkvT[:, 4 + hh, :], qkvT[:, hh, :], start=True, stop=True)
                last.then_inc(s["kk_ps"], 1)
                yield "decay"
                yield "kk"
                wait("at_sb", 1)
                for i in range(LEVELS):
                    wait("level_b", i + 1)
                    for hh in range(H):
                        last = T.matmul(B[0][:, P * hh:P * hh + P], BT[:, hh, :], X[:, hh, :], start=True, stop=True)
                    last.then_inc(s["u1_ps"], 1)
                    wait("u1_sb", i + 1)
                    for hh in range(H):
                        T.matmul(B[2][:, P * hh:P * hh + P], XT[:, hh, :], U1[:, hh, :], start=True, stop=True)
                        last = T.matmul(B[3][:, P * hh:P * hh + P], U1[:, hh, :], XT[:, hh, :], start=True, stop=True)
                    last.then_inc(s["xu_ps"], 1)
                    yield f"level{i}"
                if batch:
                    chunk("state")
                    for bank in (B[4], B[5]):
                        for hh in range(H):
                            expanded(bank[:, P * hh:P * hh + P], lambda b: SS[:, b, hh, :], True, True)
                    wait("x_level", LEVELS)
                    last = T.matmul(B[0][:, 0:4], zeros[:], g4, start=True, stop=True)
                else:
                    for hh in range(H):
                        T.matmul(B[4][:, P * hh:P * hh + P], qkvT[:, 4 + hh, :], S[:, hh, :], start=True, stop=True)
                    for hh in range(H):
                        last = T.matmul(B[5][:, P * hh:P * hh + P], qkvT[:, hh, :], S[:, hh, :], start=True, stop=True)
                last.then_inc(s["ks_ps"], 1)
                wait("rhs_sb", 1)
                wait("x_level", LEVELS)
                for hh in range(H):
                    last = T.matmul(B[0][:, P * hh:P * hh + P], XT[:, hh, :], R[:, hh, :], start=True, stop=True)
                last.then_inc(s["u_ps"], 1)
                wait("u_sb", 1)
                for hh in range(H):
                    last = T.matmul(B[1][:, P * hh:P * hh + P], QK[:, hh, :], ET[:, hh, :], start=True, stop=True)
                if batch:
                    last.then_inc(s["o_ps"], 1)
                    for hh in range(H):
                        pe.wait_ge(sup_sb_rows, 4 * layer + hh + 1)
                        if hh:
                            pe.wait_ge(sup_sb, 4 * layer + hh)
                        kd = (sc2 if hh % 2 else sc)[:, 0:NB * P].rearrange("p (b d) -> p b d", b=NB)
                        for b in range(NB):
                            last = T.matmul(B[2 + b // 4][:, P * (b % 4):P * (b % 4) + P], kd[:, b, :], ET[:, hh, :],
                                            start=True, stop=True)
                        last.then_inc(sup_ps, 1)
                else:
                    for hh in range(H):
                        last = T.matmul(B[2][:, P * hh:P * hh + P], qkv[:, 4 + hh, :], ET[:, hh, :], start=True, stop=True)
                    last.then_inc(s["o_ps"], 1)
                yield "rhs"
                yield "state"
                wait("dn_done", 1)
                wait("swq_sb", 1)
                if batch:
                    chunk("cache")
                for hb in range(4):
                    for kv in range(2):
                        hh = 4 * kv + hb
                        rows = slice(HD * kv, HD * kv + HD)
                        out = B[hh // 2][:, 2 * P * (hh % 2):2 * P * (hh % 2) + 2 * P]
                        if batch:
                            n = nz[0]
                            if kv == 0:
                                pe.wait_ge(z_made, 20 * layer + n + 1)
                            for b in range(NB):
                                last = T.matmul(out[:, 0:P], Zm[n % 2][rows, b, :], KcT[rows, b, :], start=b == 0, stop=b == NB - 1)
                            if kv == 1:
                                last.then_inc(z_used, 1)
                                nz[0] += 1
                            last = T.matmul(out[:, P:2 * P], swqT[rows, hb, :], kcat[rows, 1, :], start=True, stop=True)
                        else:
                            last = T.matmul(out, swqT[rows, hb, :], kcat[rows, :, :].rearrange("p a n -> p (a n)"), start=True, stop=True)
                last.then_inc(s["sc_ps"], 1)
                yield "scores"
                wait("sc_exp", 1)
                turn(lambda j: sc[:, P * j:P * j + P], [B[4], B[5], B[0], B[1]], "pT_ps", none)
                yield "softmax"
                for hh in range(QH):
                    wait("pT_sb", hh // 2 + 1)
                    vcol = P + HD * (hh // 4)
                    out = B[2][:, HD * hh:HD * hh + HD]
                    T.matmul(out, PT[:, 2 * hh + 1, :], kvtok[:, 1, vcol:vcol + HD], start=True, stop=False)
                    if batch:
                        expanded(out, lambda b: Vc[:, b, vcol - P:vcol - P + HD], False, True)
                    else:
                        last = T.matmul(out, PT[:, 2 * hh, :], kvtok[:, 0, vcol:vcol + HD], start=False, stop=True)
                if batch:
                    last = T.matmul(B[3][:, 0:4], zeros[:], g4, start=True, stop=True)
                last.then_inc(s["pv_ps"], 1)
                yield "pv"
                wait("mix_sb", 1)
                turn(lambda j: mix[:, P * j:P * j + P], B[3:5], "mixT_ps", none)
                wait("mixT_sb", 2)
                for i in range(2):
                    chunk(f"wo{i}")
                    for k in range(KC):
                        last = T.matmul(B[i][:], hT[:, k, :], cols(f"wo{i}")[:, k, :], start=(k == 0), stop=(k == KC - 1))
                    last.then_inc(s["wo_ps"], 1)
                yield "wo"
                wait("h2_sb", 1)
                turn(lambda j: h2[:, P * j:P * j + P], B[2:4], "h2T_ps", none)
                yield "norm2"
                wait("h2T_sb", 2)
                for i in range(4):
                    chunk(f"wq{i}")
                    for j in range(4):
                        for k in range(KC):
                            last = T.matmul(B[(4, 5, 0, 1)[i]][:, P * j:P * j + P], blocks(f"wq{i}")[:, j, k, :], hT[:, k, :],
                                            start=(k == 0), stop=(k == KC - 1))
                    last.then_inc(s["wq_ps"], 1)
                    yield f"wq{i}"
                chunk("keys")
                wait("wq_sb", 4)
                for i in range(4):
                    for j in range(4):
                        jj = 4 * i + j
                        last = T.matmul(B[2 + i][:, P * j:P * j + P], qpT[:, jj, :], keys_w[:, jj, :], start=True, stop=True)
                    last.then_inc(s["keys_ps"], 1)
                for c in ("keys", "top0", "top1", "top2", "top3", "top4", "top5"):
                    yield c

            def peer(kind, layer, tile, u):
                wait = waiter(pe, u)
                batch = kind == "batch"
                first = layer * LG + tile * PG
                half = layer * (LG // 2) + tile * (PG // 2)
                any_rhs = ident[:].unsqueeze(1).to_broadcast([P, 4, P])

                def add(k):
                    pe.wait_ge(diag_sb, first + k + 1)
                    pe.wait_ge(v_in[k % 2], (half + k // 2 + 1) * (16 * G))
                    for j in range(G):
                        for c in range(2):
                            last = T.matmul(ACC[c][:], diag[:, k % 2, j, :], vbuf[:, k % 2, j, 512 * c:512 * c + 512],
                                            start=False, stop=False, skip_group_check=True)
                    last.then_inc(v_acc, 1)
                wait("x_out", 0)
                for i in range(2):
                    T.matmul(ACC[i][:], zeros[:], any_rhs, start=True, stop=False, skip_group_check=True)
                groups = SG if batch else PG
                for k in range(groups):
                    if k:
                        add(k - 1)
                    yield
                add(groups - 1)
                for i in range(2):
                    last = T.matmul(ACC[i][:], zeros[:], any_rhs, start=False, stop=True, skip_group_check=True)
                last.then_inc(s["acc_ps"], 1)

            pe.wait_ge(const_in, 32)
            pe.wait_ge(cst, 1)
            steps(pe, dense, peer)


def constants():
    import numpy as np

    r, c = np.arange(P)[:, None], np.arange(P)[None, :]
    same = r // SLOTS == c // SLOTS
    tok = lambda n: (n % SLOTS >= HIST) & (n % SLOTS < HIST + 4)
    masks = []
    for tile in range(UNITS):
        batch = tile == TILES
        if batch:
            causal, strict = same & (c >= r), same & (c > r)
            prev, cur = tok(r) & (c > r % SLOTS - HIST), same & tok(r) & tok(c) & (c <= r)
            valid = tok(r)
        else:
            causal, strict = c >= r, c > r
            prev, cur = (c > r) & (tile > 0), c <= r
            valid = r >= 0
        levels = [(r // (2 * b) == c // (2 * b)) & (c % (2 * b) >= b) & (r % (2 * b) < b)
                  for b in (1 << i for i in range(LEVELS))]
        rows = r // SLOTS == np.arange(NB)[None, :]
        swm = np.where(np.concatenate([prev, cur], 1), 0.0, -1e30)
        masks.append(np.concatenate([causal, strict, swm, *levels, valid, rows], 1).astype(np.float32))
    sel = np.zeros((P, P), np.float32)
    for p in range(P):
        b, t = p % 32 // 4, p % 4
        sel[p, SLOTS * b + HIST + t] = 1
    return {"masks": np.stack(masks), "sel": sel, "ident": np.eye(P, dtype=np.float32),
            "iota": np.tile(np.arange(TOPK, dtype=np.float32), (P, 1))}


def layout(i):
    import numpy as np

    a = {k: np.asarray(v) for k, v in i.items()}
    w = a["w_in"]
    QW, VW = H * P, H * P
    CONV = 2 * QW + VW
    off_b = CONV + VW
    off_a = off_b + H
    off_sq = off_a + H
    off_sk = off_sq + QH * HD
    off_sv = off_sk + 2 * HD
    swq = w[:, :, off_sq:off_sk].reshape(L, D, 2, 4, HD).transpose(0, 1, 3, 2, 4).reshape(L, D, 4 * P)
    misc = np.concatenate([w[:, :, off_sk:off_sv + 2 * HD], w[:, :, off_b:off_sq]], 2)

    def blocked(m):
        return m.reshape(L, KC, P, 4, P).transpose(0, 2, 3, 1, 4).reshape(L, P, 4096)

    def columns(m):
        return m.reshape(L, KC, P, -1).transpose(0, 2, 1, 3).reshape(L, P, -1)

    big = [blocked(w[:, :, 512 * n:512 * n + 512]) for n in range(3)] + [blocked(swq), columns(w[:, :, CONV:off_b])]
    big += [columns(a["w_out"][:, :, 512 * n:512 * n + 512]) for n in range(2)]
    big += [blocked(a["peer_wq"][:, :, 512 * n:512 * n + 512]) for n in range(4)]
    xs = np.zeros((UNITS, P, D), np.float32)
    xs[:TILES] = a["x_prompt"].reshape(TILES, P, D)
    xs[TILES].reshape(NB, SLOTS, D)[:, HIST:HIST + 4] = a["x_sample"]
    rows = lambda v: np.broadcast_to(v[:, None, :], (L, P, v.shape[1]))
    off = np.broadcast_to((np.arange(L) * NEXP).astype(np.float32)[:, None, None], (L, P, 1))
    lcon = np.concatenate([rows(a["dn_a_log"]), rows(a["dn_dt_bias"]), rows(a["sw_sinks"]), rows(a["dn_norm_g"]), off], 2)
    ck, cv = a["cache_swa_k"].reshape(L, NB, P, P), a["cache_swa_v"].reshape(L, NB, P, P)
    cache = np.concatenate([ck.transpose(0, 3, 1, 2).reshape(L, P, -1), cv.transpose(0, 2, 1, 3).reshape(L, P, -1)], 2)
    c9 = np.concatenate([a["c_prompt"], a["c_sample"]], 0)
    got = {
        "xs": xs, "cT": c9.T.reshape(KC, P, 9).transpose(1, 0, 2).reshape(P, -1),
        "w_ada": a["w_ada"].reshape(L, KC, P, 12, 512).transpose(0, 3, 2, 1, 4).reshape(L, 12, P, 4096),
        "b_ada": a["b_ada"], "g1n": a["norm1_g"], "g2n": a["norm2_g"], "gfin": a["final_norm_g"],
        "w_big": np.stack(big, 1), "w_misc": columns(misc),
        "keysT": a["peer_keys"].transpose(0, 4, 1, 2, 3).reshape(L, P, -1),
        "state": a["state_delta"].transpose(0, 3, 1, 2, 4), "cache": cache,
        "cache_k": ck, "cache_v": cv,
        "hist": a["state_conv"].reshape(L, NB, HIST, CH, P).transpose(0, 4, 3, 1, 2),
        "cw": a["conv_w"].reshape(L, 4, CH, P).transpose(0, 3, 2, 1), "lcon": lcon,
        "peer_u": a["peer_u"].reshape(L * NEXP, D), "peer_v": a["peer_v"].reshape(L * NEXP, D),
        **constants(),
    }
    return {k: np.ascontiguousarray(v) for k, v in got.items()}


OUTS = {
    "y": (UNITS, P, D), "delta_p": (L, P, H, P), "conv_p": (L, P, CH, HIST), "kv_p": (L, P, 2 * P),
    "delta_s": (L, P, NB, H, P), "conv_s": (L, P, CH, NB, HIST), "k_s": (L, NB, P, P), "v_s": (L, NB, P, P),
}
SCRATCH = {"xbuf": ((L + 1, UNITS, P, D), F32), "mod": ((L, 9, 6 * D), F32), "b_idx": ((P, EXPERTS), U32),
           "b_gate": ((P, EXPERTS), F32), "b_h2": ((P, D), F32)}


def kernel(**inputs):
    import numpy as np
    import concourse.bacc as bacc
    from concourse.bass_utils import run_bass_kernel_spmd as run

    nc = bacc.Bacc("TRN2", target_bir_lowering=False, num_devices=1)
    arrays = layout(inputs)
    ins = {k: nc.dram_tensor("in_" + k, v.shape, mybir.dt.from_np(v.dtype), kind="ExternalInput").ap() for k, v in arrays.items()}
    outs = {k: nc.dram_tensor("out_" + k, shape, F32, kind="ExternalOutput").ap() for k, shape in OUTS.items()}
    outs |= {k: nc.dram_tensor("dram_" + k, shape, dt).ap() for k, (shape, dt) in SCRATCH.items()}
    trunk(nc, ins, outs)
    r = run(nc, [{"in_" + k: v for k, v in arrays.items()}], core_ids=[0]).results[0]
    r = {k: r["out_" + k] for k in OUTS}
    y = r["y"]
    conv_s = r["conv_s"].transpose(0, 3, 4, 2, 1).reshape(L, NB, HIST, CH * P)
    k_p, v_p = (np.ascontiguousarray(r["kv_p"][:, :, n * P:(n + 1) * P]).reshape(L, 1, P, 2, HD) for n in range(2))
    return (
        y[:TILES].reshape(1, TILES * P, D),
        np.ascontiguousarray(y[TILES].reshape(NB, SLOTS, D)[:, HIST:HIST + 4]),
        np.ascontiguousarray(r["delta_p"].transpose(0, 2, 1, 3)).reshape(L, 1, H, P, P),
        np.ascontiguousarray(r["conv_p"].transpose(0, 3, 2, 1)).reshape(L, 1, HIST, CH * P),
        k_p, v_p,
        np.ascontiguousarray(r["delta_s"].transpose(0, 2, 3, 1, 4)),
        np.ascontiguousarray(conv_s),
        r["k_s"].reshape(L, NB, P, 2, HD), r["v_s"].reshape(L, NB, P, 2, HD),
    )
```
